# Optimizing a Trainium2 kernel written in Bass

```python
import jax, jax.numpy as jnp
from jax import lax
import numpy as np

D_MODEL = 1024
BATCH = 1
SEQ = 1024
DEPTH = 1

CHUNK = 64
Q_BLOCK = 128
D_MIX = D_MODEL
SB_WIDTH = D_MIX // 2
SB_HEAD_DIM = 64
SB_HEADS = SB_WIDTH // SB_HEAD_DIM
GLA_WIDTH = D_MIX - SB_WIDTH
GLA_HEADS = 4
GLA_VAL_DIM = GLA_WIDTH // GLA_HEADS
GLA_KEY_DIM = GLA_VAL_DIM // 2
GLA_QK_WIDTH = GLA_HEADS * GLA_KEY_DIM
GLA_GATE_RANK = 16
GLA_GATE_TAU = 16.0
IN_SIZES = (SB_WIDTH, SB_WIDTH, SB_WIDTH, GLA_QK_WIDTH, GLA_QK_WIDTH, GLA_WIDTH, GLA_WIDTH, GLA_GATE_RANK)
IN_DIM = sum(IN_SIZES)
N_GROUPS = 4
EXPERTS_PER_GROUP = 8
N_EXPERTS = N_GROUPS * EXPERTS_PER_GROUP
TOP_K = 2
D_EXPERT = D_MODEL // 2
EXPERT_BLOCK = 128
EPS = 1e-6

kernel_name = 'hymba_sb_gla_hiermoe_block'

def rms_norm(x, g):
    xf = x.astype(jnp.float32)
    y = xf * lax.rsqrt(jnp.mean(xf * xf, axis=-1, keepdims=True) + EPS)
    return (y * g.astype(jnp.float32)).astype(x.dtype)

def split_cols(a, sizes):
    out, off = [], 0
    for s in sizes:
        out.append(a[..., off:off + s])
        off += s
    return out

def stick_breaking_attention(q, k, v):
    B, T, H, Dh = q.shape
    scale = Dh ** -0.5
    outs = []
    for i in range(T // Q_BLOCK):
        q0 = i * Q_BLOCK
        kend = q0 + Q_BLOCK
        qb = q[:, q0:kend]
        kb = k[:, :kend]
        vb = v[:, :kend]
        z = jnp.einsum('bqhd,bshd->bhqs', qb, kb).astype(jnp.float32) * scale
        t_idx = q0 + jnp.arange(Q_BLOCK)[:, None]
        s_idx = jnp.arange(kend)[None, :]
        strict = s_idx < t_idx
        log_beta = jax.nn.log_sigmoid(z)
        log_1mb = jnp.where(strict, jax.nn.log_sigmoid(-z), 0.0)
        tail = lax.cumsum(log_1mb, axis=3, reverse=True) - log_1mb
        a = jnp.where(strict, jnp.exp(log_beta + tail), 0.0)
        outs.append(jnp.einsum('bhqs,bshd->bqhd', a.astype(vb.dtype), vb))
    return jnp.concatenate(outs, axis=1)

def gla_chunked(q, k, v, log_g):
    B, T, H, Dk = q.shape
    Dv = v.shape[-1]
    nc = T // CHUNK

    def to_chunks(a):
        return jnp.moveaxis(a.reshape(B, nc, CHUNK, H, a.shape[-1]), 1, 0)

    def step(S, inp):
        qi, ki, vi, gi = inp
        lcum = jnp.cumsum(gi.astype(jnp.float32), axis=1)
        total = lcum[:, -1]
        k_dec = ki.astype(jnp.float32) * jnp.exp(total[:, None] - lcum)
        S = jnp.exp(total)[..., None] * S + jnp.einsum('bchk,bchv->bhkv', k_dec, vi.astype(jnp.float32))
        o = jnp.einsum('bchk,bhkv->bchv', qi.astype(jnp.float32), S)
        return S, o

    S0 = jnp.zeros((B, H, Dk, Dv), jnp.float32)
    _, o = lax.scan(step, S0, (to_chunks(q), to_chunks(k), to_chunks(v), to_chunks(log_g)))
    return jnp.moveaxis(o, 0, 1).reshape(B, T, H, Dv).astype(v.dtype)

def hierarchical_moe(h, w_grp, b_grp, w_exp, b_exp, w_gate, w_up, w_down):
    B, T, D = h.shape
    N = B * T
    hf = h.reshape(N, D)
    grp_logits = (hf @ w_grp + b_grp).astype(jnp.float32)
    grp_prob = jax.nn.softmax(grp_logits, axis=-1)
    g_sel = jnp.argmax(grp_logits, axis=-1).astype(jnp.int32)
    p_grp = jnp.take_along_axis(grp_prob, g_sel[:, None], axis=-1)
    exp_logits = (hf @ w_exp + b_exp).astype(jnp.float32).reshape(N, N_GROUPS, EXPERTS_PER_GROUP)
    exp_logits = jnp.take_along_axis(exp_logits, g_sel[:, None, None], axis=1)[:, 0]
    p_exp = jax.nn.softmax(exp_logits, axis=-1)
    top_p, top_local = lax.top_k(p_exp, TOP_K)
    top_p = top_p / jnp.sum(top_p, axis=-1, keepdims=True)
    gates = p_grp * top_p
    expert_id = g_sel[:, None] * EXPERTS_PER_GROUP + top_local.astype(jnp.int32)

    nk = N * TOP_K
    e_flat = expert_id.reshape(nk)
    tok_flat = jnp.repeat(jnp.arange(N, dtype=jnp.int32), TOP_K)
    gate_flat = gates.reshape(nk)
    order = jnp.argsort(e_flat)
    e_sorted = e_flat[order]
    counts = jnp.zeros((N_EXPERTS,), jnp.int32).at[e_flat].add(1)
    padded = (counts + EXPERT_BLOCK - 1) // EXPERT_BLOCK * EXPERT_BLOCK
    start = jnp.cumsum(counts) - counts
    pend = jnp.cumsum(padded)
    pstart = pend - padded
    rank = jnp.arange(nk, dtype=jnp.int32) - start[e_sorted]
    dest = pstart[e_sorted] + rank
    n_blocks = -(-nk // EXPERT_BLOCK) + N_EXPERTS
    R = n_blocks * EXPERT_BLOCK
    row_tok = jnp.full((R,), N, jnp.int32).at[dest].set(tok_flat[order])
    row_gate = jnp.zeros((R,), hf.dtype).at[dest].set(gate_flat[order].astype(hf.dtype))
    hf_pad = jnp.concatenate([hf, jnp.zeros((1, D), hf.dtype)], axis=0)
    rows = hf_pad[row_tok].reshape(n_blocks, EXPERT_BLOCK, D)
    block_start = jnp.arange(n_blocks, dtype=jnp.int32) * EXPERT_BLOCK
    block_expert = jnp.minimum(jnp.sum(block_start[:, None] >= pend[None, :], axis=1), N_EXPERTS - 1).astype(jnp.int32)

    def expert_block(args):
        xb, e = args
        return (jax.nn.silu(xb @ w_gate[e]) * (xb @ w_up[e])) @ w_down[e]

    y_rows = lax.map(expert_block, (rows, block_expert)).reshape(R, D)
    y = jnp.zeros((N + 1, D), hf.dtype).at[row_tok].add(y_rows * row_gate[:, None])
    return y[:N].reshape(B, T, D)

def setup_inputs(seed: int = 0) -> dict:
    key = jax.random.key(seed)
    ks = jax.random.split(key, 18)
    f = jnp.float32

    def nrm(k, shape, scale):
        return jax.random.normal(k, shape, f) * scale

    def gain(k, shape):
        return 1.0 + 0.02 * jax.random.normal(k, shape, f)

    L = DEPTH
    return {
        'x': jax.random.normal(ks[0], (BATCH, SEQ, D_MODEL), f),
        'attn_norm_g': gain(ks[1], (L, D_MODEL)),
        'w_in': nrm(ks[2], (L, D_MODEL, IN_DIM), D_MODEL ** -0.5),
        'sb_q_norm_g': gain(ks[3], (L, SB_HEAD_DIM)),
        'sb_k_norm_g': gain(ks[4], (L, SB_HEAD_DIM)),
        'sb_out_norm_g': gain(ks[5], (L, SB_HEADS, SB_HEAD_DIM)),
        'gla_gate_w2': nrm(ks[6], (L, GLA_GATE_RANK, GLA_QK_WIDTH), GLA_GATE_RANK ** -0.5),
        'gla_gate_b': nrm(ks[7], (L, GLA_QK_WIDTH), 0.1),
        'gla_out_norm_g': gain(ks[8], (L, GLA_VAL_DIM)),
        'w_out': nrm(ks[9], (L, D_MIX, D_MODEL), D_MIX ** -0.5),
        'ffn_norm_g': gain(ks[10], (L, D_MODEL)),
        'router_group_w': nrm(ks[11], (L, D_MODEL, N_GROUPS), D_MODEL ** -0.5),
        'router_group_b': nrm(ks[12], (L, N_GROUPS), 0.01),
        'router_expert_w': nrm(ks[13], (L, D_MODEL, N_EXPERTS), D_MODEL ** -0.5),
        'router_expert_b': nrm(ks[14], (L, N_EXPERTS), 0.01),
        'expert_w_gate': nrm(ks[15], (L, N_EXPERTS, D_MODEL, D_EXPERT), D_MODEL ** -0.5),
        'expert_w_up': nrm(ks[16], (L, N_EXPERTS, D_MODEL, D_EXPERT), D_MODEL ** -0.5),
        'expert_w_down': nrm(ks[17], (L, N_EXPERTS, D_EXPERT, D_MODEL), D_EXPERT ** -0.5),
    }

def reference(x, attn_norm_g, w_in, sb_q_norm_g, sb_k_norm_g, sb_out_norm_g, gla_gate_w2, gla_gate_b,
              gla_out_norm_g, w_out, ffn_norm_g, router_group_w, router_group_b, router_expert_w,
              router_expert_b, expert_w_gate, expert_w_up, expert_w_down):
    B, T, _ = x.shape
    h = x
    for l in range(DEPTH):
        u = rms_norm(h, attn_norm_g[l])
        proj = u @ w_in[l]
        sq, sk, sv, gq, gk, gv, gr, glr = split_cols(proj, IN_SIZES)

        sq = rms_norm(sq.reshape(B, T, SB_HEADS, SB_HEAD_DIM), sb_q_norm_g[l])
        sk = rms_norm(sk.reshape(B, T, SB_HEADS, SB_HEAD_DIM), sb_k_norm_g[l])
        sv = sv.reshape(B, T, SB_HEADS, SB_HEAD_DIM)
        sb = stick_breaking_attention(sq, sk, sv)
        sb = rms_norm(sb, sb_out_norm_g[l]).reshape(B, T, SB_WIDTH)

        gq = gq.reshape(B, T, GLA_HEADS, GLA_KEY_DIM) * (GLA_KEY_DIM ** -0.5)
        gk = gk.reshape(B, T, GLA_HEADS, GLA_KEY_DIM)
        gv = gv.reshape(B, T, GLA_HEADS, GLA_VAL_DIM)
        log_g = jax.nn.log_sigmoid((glr @ gla_gate_w2[l] + gla_gate_b[l]).astype(jnp.float32)) / GLA_GATE_TAU
        log_g = log_g.reshape(B, T, GLA_HEADS, GLA_KEY_DIM)
        go = gla_chunked(gq, gk, gv, log_g)
        go = rms_norm(go, gla_out_norm_g[l]) * jax.nn.silu(gr.reshape(B, T, GLA_HEADS, GLA_VAL_DIM))
        go = go.reshape(B, T, GLA_WIDTH)

        h = h + jnp.concatenate([sb, go], axis=-1) @ w_out[l]

        v = rms_norm(h, ffn_norm_g[l])
        h = h + hierarchical_moe(v, router_group_w[l], router_group_b[l], router_expert_w[l],
                                 router_expert_b[l], expert_w_gate[l], expert_w_up[l], expert_w_down[l])
    return h


_drawn_inputs = setup_inputs


def setup_inputs(seed=0):
    import zlib

    import numpy as np

    out = dict(_drawn_inputs(seed))
    spreads = {}
    factors = {'sb_q_norm_g': 3.906,
     'sb_k_norm_g': 5.407,
     'gla_out_norm_g': 9.402,
     'router_group_b': 11.655,
     'router_expert_b': 16.17,
     'sb_out_norm_g': 4.951,
     'ffn_norm_g': 3.273}
    for name, (base, spread) in spreads.items():
        noise = np.random.default_rng([zlib.crc32(name.encode()), seed]).standard_normal(out[name].shape)
        drawn = base * np.exp(spread * noise) if base else spread * noise
        out[name] = __import__('jax').numpy.asarray(drawn.astype(out[name].dtype))
    for name, factor in factors.items():
        out[name] = (out[name] * factor).astype(out[name].dtype)
    return out
```

```python
import numpy as np
import concourse.bass as bass
from concourse import mybir
from contextlib import ExitStack

P = 128
D = 1024
T = 1024
TILES = T // P
KT = D // P
HALF = 512
SB_HEADS, SB_DIM = 8, 64
GLA_HEADS, GLA_K, GLA_V = 4, 64, 128
CHUNK = 64
RANK = 16
TAU = 16.0
N_GROUPS, PER_GROUP = 4, 8
EXPERTS = N_GROUPS * PER_GROUP
FF = 512
FT = FF // P
LOGITS = N_GROUPS + EXPERTS
EPS = 1e-6
MAX_BLOCKS = 48
SLOTS = MAX_BLOCKS * P
NEG = -1e30
GUARD = 80.0
CAP = 16.0
PIECE = 2048
RAW = 6
SPLIT = 6
COLS = {"q": 0, "k": 512, "v": 1024, "gqk": 1536, "gv": 2048, "gr": 2560, "glr": 3072}
ORDER = ["gv", "gr", "gqk", "q", "k", "v"]


def hybrid_block_kernel(nc, x, attn_norm_g, w_in, sb_q_norm_g, sb_k_norm_g, sb_out_norm_g, gla_gate_w2,
                        gla_gate_b, gla_out_norm_g, w_out, ffn_norm_g, router_group_w, router_group_b,
                        router_expert_w, router_expert_b, expert_w_gate, expert_w_up, expert_w_down, out):
    fp32, f32r, bf16, u32, i32 = (mybir.dt.float32, mybir.dt.float32r, mybir.dt.bfloat16, mybir.dt.uint32,
                                  mybir.dt.int32)
    ALU, ACT, AX = mybir.AluOpType, mybir.ActivationFunctionType, mybir.AxisListType
    ADD, SUB, MUL = ALU.add, ALU.subtract, ALU.mult

    gv_dram = nc.dram_tensor("gv_dram", (TILES, P, HALF), fp32, kind="Internal").ap()
    gr_dram = nc.dram_tensor("gr_dram", (TILES, P, HALF), fp32, kind="Internal").ap()
    v_dram = nc.dram_tensor("v_dram", (T, D), fp32, kind="Internal").ap()
    table_dram = nc.dram_tensor("table_dram", (SLOTS, 2), u32, kind="Internal").ap()

    x_t = x[0].rearrange("(t p) d -> t p d", p=P)
    out_rows = out[0]
    out_t = out_rows.rearrange("(t p) d -> t p d", p=P)
    w_in_v = w_in[0].rearrange("(p k) n -> p k n", k=KT)
    w_out_v = w_out[0].rearrange("(k p) n -> p k n", p=P)
    gate_v = expert_w_gate[0].rearrange("e (p k) n -> e p (k n)", k=KT)
    up_v = expert_w_up[0].rearrange("e (p k) n -> e p (k n)", k=KT)
    down_v = expert_w_down[0].rearrange("e (p k) n -> e p (k n)", k=FT)

    ctx = ExitStack()
    with ctx:
        def const(name, shape, dt=fp32):
            return ctx.enter_context(nc.sbuf_tensor(name, shape, dt))

        def sem(name):
            return ctx.enter_context(nc.semaphore(name))

        ident = const("ident", [P, P])
        ident_b = const("ident_b", [P, P], bf16)
        causal_neg = const("causal_neg", [P, P], bf16)
        tri_f = const("tri_f", [P, P])
        tri_neg = const("tri_neg", [P, P], f32r)
        ones_neg = const("ones_neg", [P, P])
        head_mean = const("head_mean", [P, P])
        suffix = const("suffix", [P, P])
        chunk_sel = const("chunk_sel", [P, 2])
        before = const("before", [P, P], bf16)
        ones_b = const("ones_b", [P, P], bf16)
        iota = const("iota", [P, EXPERTS])
        eps_col = const("eps_col", [P, 1])
        gate_w2 = const("gate_w2", [RANK + 1, 256])
        gla_gain = const("gla_gain", [P, GLA_V])
        router_bias = const("router_bias", [P, LOGITS])
        q_gain = const("q_gain", [P, 1])
        k_gain = const("k_gain", [P, 1])
        o_gain = const("o_gain", [P, SB_HEADS // 2])
        router_w = const("router_w", [P, KT, LOGITS])
        glr = const("glr", [P, TILES, RANK])
        glr_t = const("glr_t", [RANK + 1, P])
        stat = const("stat", [P, 16])
        grp_logits = const("grp_logits", [P, 8])
        top_val = const("top_val", [P, 2, 8])
        top_idx = const("top_idx", [P, 2, 8], u32)
        chosen = const("chosen", [P, TILES, 2, EXPERTS], bf16)
        chosen_any = const("chosen_any", [P, TILES, EXPERTS], bf16)
        expert_of = const("expert_of", [P, TILES, 2])
        payload = const("payload", [P, TILES, 2, 2], u32)
        address = const("address", [P, TILES * 2], u32)
        control = const("control", [P, 2 + 16], i32)
        table = const("table", [P, MAX_BLOCKS, 2], u32)
        exp_logits = const("exp_logits", [P, EXPERTS])
        masked = const("masked", [P, EXPERTS])
        sel_logits = const("sel_logits", [P, 8])
        r_small = const("r_small", [P, 18])
        table_fill = const("table_fill", [P, MAX_BLOCKS * 2], u32)
        gather_idx = const("gather_idx", [P, 1], u32)
        scatter_row = const("scatter_row", [P, 2], u32)

        base = (nc.sbuf_usable_end - nc.sbuf_bytes_remaining + 63) // 64 * 64
        KB = 1024
        R1, R2, R3 = base, base + 64 * KB, base + 128 * KB
        RAWS = R3 + 20 * KB
        assert RAWS + 48 * KB <= nc.sbuf_usable_end, (base, nc.sbuf_usable_end)

        def at(name, offset, shape, dt=fp32):
            return nc.alloc_sbuf_tensor_at(name, shape, dt, offset=offset)

        q_t = at("q_t", R1, [P, 4, T])
        k_t = at("k_t", R1 + 16 * KB, [P, 4, T])
        v_s = at("v_s", R1 + 32 * KB, [P, TILES, HALF])
        gq_t = at("gq_t", R1 + 48 * KB, [P, 2, T])
        gk_t = at("gk_t", R1 + 56 * KB, [P, 2, T])
        u_h = at("u_h", R2, [P, KT, T], f32r)
        u_l = at("u_l", R2 + 32 * KB, [P, KT, T], f32r)
        win_raw = [at(f"win_raw{i}", R3 + 8 * KB * i, [P, PIECE]) for i in range(2)]
        win_h = [at(f"win_h{i}", R3 + (16 + 8 * i) * KB, [P, 4, HALF], f32r) for i in range(2)]
        win_l = [at(f"win_l{i}", R3 + (32 + 8 * i) * KB, [P, 4, HALF], f32r) for i in range(2)]
        x_in = [at(f"x_in{i}", R1 + 4 * KB * i, [P, D]) for i in range(TILES)]
        u_row = [at(f"u_row{i}", R1 + (32 + 4 * i) * KB, [P, D]) for i in range(2)]
        squares = at("squares", R1 + 40 * KB, [P, D])
        gain1 = at("gain1", R1 + 44 * KB, [P, D])
        spill = [at(f"spill{i}", R3 + (64 + 2 * i) * KB, [P, HALF]) for i in range(2)]
        glr_raw = at("glr_raw", R3 + 48 * KB, [P, KT, RANK])
        glr_h = at("glr_h", R3 + 49 * KB, [P, KT, RANK], f32r)
        glr_l = at("glr_l", R3 + 50 * KB, [P, KT, RANK], f32r)
        mix_h = at("mix_h", R2, [P, KT, T], f32r)
        mix_l = at("mix_l", R2 + 32 * KB, [P, KT, T], f32r)
        place = [R3]

        def nxt(name, n, dt=fp32, shape=None):
            t = at(name, place[0], shape or [P, n], dt)
            place[0] += n * 4
            return t

        soft = [nxt(f"soft{i}", HALF) for i in range(2)]
        sp = [nxt(f"sp{i}", HALF) for i in range(3)]
        sp_h = [nxt(f"sp_h{i}", HALF, f32r) for i in range(3)]
        sp_l = [nxt(f"sp_l{i}", HALF, f32r) for i in range(3)]
        later = [nxt(f"later{i}", HALF) for i in range(3)]
        prob = [nxt(f"prob{i}", HALF) for i in range(2)]
        o_s = nxt("o_s", HALF)
        sq = nxt("sq", HALF)
        rs = nxt("rs", HALF)
        gv_s = nxt("gv_s", HALF)
        gr_s = nxt("gr_s", HALF)
        gsig = nxt("gsig", HALF)
        gk_s = nxt("gk_s", 256)
        k_dec = nxt("k_dec", 256)
        log_g = nxt("log_g", 256)
        go = nxt("go", HALF)
        state = [nxt(f"state{i}", HALF, shape=[P, 2, 256]) for i in range(3)]
        gstat = nxt("gstat", 32)
        assert place[0] <= R3 + 60 * KB, place[0] - R3
        wo_h = at("wo_h", R1, [P, KT, D], f32r)
        wo_l = at("wo_l", R1 + 32 * KB, [P, KT, D], f32r)
        h_row = [at(f"h_row{i}", R3 + 4 * KB * i, [P, D]) for i in range(2)]
        v_row = at("v_row", R3 + 8 * KB, [P, D])
        v_t = at("v_t", R3 + 12 * KB, [P, KT, P])
        gain2 = at("gain2", R3 + 16 * KB, [P, D])
        raw = [at(f"raw{i}", RAWS + (40 * KB if i == 0 else 8 * KB * (i - 1)), [P, PIECE]) for i in range(RAW)]
        ew_h = [at(f"ew_h{i}", R1 + 16 * KB * i, [P, PIECE], f32r) for i in range(SPLIT)]
        ew_l = [at(f"ew_l{i}", R1 + 16 * KB * i + 8 * KB, [P, PIECE], f32r) for i in range(SPLIT)]
        M = R1 + 96 * KB
        xb = at("xb", M, [P, D])
        xb_h = at("xb_h", M + 4 * KB, [P, KT, P], f32r)
        xb_l = at("xb_l", M + 8 * KB, [P, KT, P], f32r)
        silu = at("silu", M + 12 * KB, [P, FF])
        act_row = at("act_row", M + 14 * KB, [P, FF])
        a_h = at("a_h", M + 16 * KB, [P, FT, P], f32r)
        a_l = at("a_l", M + 18 * KB, [P, FT, P], f32r)
        y_row = at("y_row", M + 20 * KB, [P, D])
        place[0] = M + 24 * KB
        big = nxt("big", TILES * 2 * EXPERTS)
        rank = nxt("rank", 16)
        extra = nxt("extra", 16)
        level = nxt("level", 16)
        blk = nxt("blk", 16)
        tmp16 = nxt("tmp16", 16)
        n_extra = nxt("n_extra", EXPERTS)
        end_extra = nxt("end_extra", EXPERTS)
        start_extra = nxt("start_extra", EXPERTS)
        ctl_f = nxt("ctl_f", 18)
        assert place[0] <= R1 + 128 * KB

        bank = [ctx.enter_context(nc.psum_tensor(f"bank{i}", [P, HALF], fp32)) for i in range(8)]

        fixed = sem("fixed")
        consts_in = sem("consts_in")
        gain_in = sem("gain_in")
        xs = [sem(f"x_loaded{i}") for i in range(TILES)]
        fill_ready = sem("fill_ready")
        small = sem("small")
        asmall = sem("asmall")
        psmall = sem("psmall")
        square_done, mean_done, rstd_done = sem("square_done"), sem("mean_done"), sem("rstd_done")
        u_ready, u_turned, uh_ready, ul_ready = sem("u_ready"), sem("u_turned"), sem("uh_ready"), sem("ul_ready")
        win_in = [sem(f"win_loaded{i}") for i in range(2)]
        win_h_ready, win_l_ready, win_used = sem("win_h_ready"), sem("win_l_ready"), sem("win_used")
        unit_done, unit_out = sem("unit_done"), sem("unit_out")
        spilled = [sem(f"spilled{i}") for i in range(2)]
        glr_in, glr_split, glr_done, glr_out = sem("glr_in"), sem("glr_split"), sem("glr_done"), sem("glr_out")
        qk_done, cap_done, ln_done = sem("qk_done"), sem("cap_done"), sem("ln_done")
        sp_done, spl_done, later_done = sem("sp_done"), sem("spl_done"), sem("later_done")
        tail_done, prob_done, pv_done = sem("tail_done"), sem("prob_done"), sem("pv_done")
        sq_done, ms_done, rs_done = sem("sq_done"), sem("ms_done"), sem("rs_done")
        q_normed, mix_ready = sem("q_normed"), sem("mix_ready")
        gvr_in, g_turned, g_turned_out, g_logit = sem("gvr_in"), sem("g_turned"), sem("g_turned_out"), sem("g_logit")
        g_cap, g_ln, g_log, g_decay, g_exp = sem("g_cap"), sem("g_ln"), sem("g_log"), sem("g_decay"), sem("g_exp")
        g_kdec, g_kv, g_state, g_o = sem("g_kdec"), sem("g_kv"), sem("g_state"), sem("g_o")
        g_rcap, g_sig, g_silu, g_gain, g_sq, g_ms, g_rs = (sem("g_rcap"), sem("g_sig"), sem("g_silu"), sem("g_gain"), sem("g_sq"),
                                                   sem("g_ms"), sem("g_rs"))
        g_go, g_got, g_mixh, g_mixl = sem("g_go"), sem("g_got"), sem("g_mixh"), sem("g_mixl")
        raw_in = [sem(f"raw_loaded{i}") for i in range(RAW)]
        wo_h_ready, wo_l_ready = sem("wo_h_ready"), sem("wo_l_ready")
        hx = [sem(f"h_x_loaded{i}") for i in range(2)]
        gain2_in = sem("gain2_in")
        wo_done, h_ready, h_square, h_mean, h_rstd, v_ready = (sem("wo_done"), sem("h_ready"), sem("h_square"),
                                                               sem("h_mean"), sem("h_rstd"), sem("v_ready"))
        h_stored = [sem(f"h_stored{i}") for i in range(2)]
        v_stored = sem("v_stored")
        v_turned, vt_ready, logit_done, logit_out = (sem("v_turned"), sem("vt_ready"), sem("logit_done"),
                                                     sem("logit_out"))
        r_max, r_exp, r_diff, r_ratio, routed = sem("r_max"), sem("r_exp"), sem("r_diff"), sem("r_ratio"), sem("routed")
        ranked, addressed, table_init = sem("ranked"), sem("addressed"), sem("table_init")
        table_written, table_in = sem("table_written"), sem("table_in")
        ew_h_ready, ew_l_ready, ew_used = sem("ew_h_ready"), sem("ew_l_ready"), sem("ew_used")
        rows_in, idx_ready, x_turned, xh_ready, xl_ready = (sem("rows_in"), sem("idx_ready"), sem("x_turned"),
                                                            sem("xh_ready"), sem("xl_ready"))
        xb_clear = sem("xb_clear")
        gate_done, up_done, silu_done, act_done = sem("gate_done"), sem("up_done"), sem("silu_done"), sem("act_done")
        a_turned, ah_ready, al_ready, down_done = sem("a_turned"), sem("ah_ready"), sem("al_ready"), sem("down_done")
        row_ready, y_ready, y_added = sem("row_ready"), sem("y_ready"), sem("y_added")

        N_CONSTS = 12
        units = []
        for pair in range(4):
            for qc in (1, 0):
                for hd in (2 * pair, 2 * pair + 1):
                    js = list(range(4 * qc + 3, -1, -1))
                    for j in js:
                        q0 = HALF * qc
                        units.append(dict(pair=pair, qc=qc, hd=hd, j=j, first=j == js[0], last=j == 0,
                                          lo=max(P * j, q0) - q0, diag=P * j >= q0))
        NU = len(units)
        PER_PAIR = NU // 4
        GROUP_END = {PER_PAIR * p + e: 2 * p + g for p in range(4) for g, e in enumerate((15, 23))}
        WINDOW = NU // TILES
        SLOT_END = NU + 9
        QN = 4
        MS_QK0 = 7

        def piece_slot(n):
            return n % RAW, n // RAW + 1

        def laters(n):
            return sum(not u["last"] for u in units[:n])

        block = ctx.enter_context(nc.Block())

        def norm_event(s):
            p, r = divmod(s, PER_PAIR)
            if p < 3 and s < NU and MS_QK0 <= r < MS_QK0 + 3 * QN and (r - MS_QK0) % 3 == 0:
                return p + 1, (r - MS_QK0) // 3
            return None

        norm_order = {("qk", 0, b): b for b in range(QN)}
        for s in range(SLOT_END):
            if s >= 5 and s - 5 in GROUP_END:
                norm_order[("o", GROUP_END[s - 5])] = len(norm_order)
            if s >= 1 and norm_event(s - 1):
                norm_order[("qk", *norm_event(s - 1))] = len(norm_order)

        def qk_block(b, pair):
            src = (q_t, k_t)[b // 2]
            return src[:, pair, HALF * (b % 2):HALF * (b % 2) + HALF]

        @block.sync
        def _(sp_e):
            def load_win(n):
                c0 = COLS[ORDER[n // 2]]
                sp_e.dma_start(win_raw[n % 2][:, :].rearrange("p (k n) -> p k n", n=HALF),
                               w_in_v[:, 4 * (n % 2):4 * (n % 2) + 4, c0:c0 + HALF]).then_inc(win_in[n % 2], 16)

            for t in range(TILES):
                sp_e.dma_start(x_in[t][:, :], x_t[t]).then_inc(xs[t], 16)
                if t == 0:
                    sp_e.dma_start(gain1[:, :], attn_norm_g[0:1, :].partition_broadcast(P)).then_inc(gain_in, 16)
            load_win(0)
            load_win(1)
            sp_e.dma_start(glr_raw[:, :, :], w_in_v[:, :, COLS["glr"]:COLS["glr"] + RANK]).then_inc(glr_in, 16)
            sp_e.wait_ge(fill_ready, 1)
            sp_e.dma_start(table_dram.rearrange("(p b) c -> p (b c)", b=MAX_BLOCKS), table_fill[:, :]).then_inc(table_init, 16)
            c = [0]

            def load(dst, src):
                c[0] += 1
                sp_e.dma_start(dst, src, allow_slow_non_contiguous=True).then_inc(consts_in, 16)

            load(gate_w2[0:RANK, :], gla_gate_w2[0])
            load(gate_w2[RANK:RANK + 1, :], gla_gate_b)
            load(gla_gain[:, :], gla_out_norm_g.partition_broadcast(P))
            load(router_bias[:, 0:N_GROUPS], router_group_b.partition_broadcast(P))
            load(router_bias[:, N_GROUPS:LOGITS], router_expert_b.partition_broadcast(P))
            for r in range(2):
                load(q_gain[SB_DIM * r:SB_DIM * (r + 1), :], sb_q_norm_g.rearrange("a d -> d a"))
                load(k_gain[SB_DIM * r:SB_DIM * (r + 1), :], sb_k_norm_g.rearrange("a d -> d a"))
                load(o_gain[SB_DIM * r:SB_DIM * (r + 1), :],
                     sb_out_norm_g[0].rearrange("(a b) d -> b d a", b=2)[r])
            load(router_w[:, :, 0:N_GROUPS], router_group_w[0].rearrange("(p k) n -> p k n", k=KT))
            sp_e.dma_start(router_w[:, :, N_GROUPS:LOGITS],
                           router_expert_w[0].rearrange("(p k) n -> p k n", k=KT)).then_inc(consts_in, 16)
            assert c[0] == N_CONSTS
            for n in range(2, 2 * len(ORDER)):
                sp_e.wait_ge(win_l_ready, n - 1)
                load_win(n)
            sp_e.wait_ge(glr_done, 1)
            sp_e.wait_ge(glr_out, 1)
            for i in range(2):
                sp_e.wait_ge(spilled[i], 16 * TILES)
            sp_e.dma_start(raw[0][:, :].rearrange("p (k n) -> p k n", n=D), w_out_v[:, 0:2, :]).then_inc(raw_in[0], 16)
            for t in range(TILES):
                if t:
                    sp_e.wait_ge(g_kv, 2 * t)
                    sp_e.wait_ge(g_silu, t)
                sp_e.dma_start(gv_s[:, :], gv_dram[t]).then_inc(gvr_in, 16)
                sp_e.dma_start(gr_s[:, :], gr_dram[t]).then_inc(gvr_in, 16)
            sp_e.wait_ge(mix_ready, 8)
            sp_e.wait_ge(g_mixh, TILES)
            sp_e.wait_ge(g_mixl, TILES)
            for n in range(1, 4):
                sp_e.dma_start(raw[n][:, :].rearrange("p (k n) -> p k n", n=D),
                               w_out_v[:, 2 * n:2 * n + 2, :]).then_inc(raw_in[n], 16)
                if n < 3:
                    sp_e.dma_start(h_row[n - 1][:, :], x_t[n - 1]).then_inc(hx[n - 1], 16)
            sp_e.dma_start(gain2[:, :], ffn_norm_g.partition_broadcast(P)).then_inc(gain2_in, 16)

            def load_piece(slot, src):
                sp_e.dma_start(raw[slot][:, :], src).then_inc(raw_in[slot], 16)

            def gate_up(e, j):
                v = (gate_v, up_v)[j // 2]
                return v[e][:, PIECE * (j % 2):PIECE * (j % 2 + 1)]

            for j in range(4):
                if j >= 2:
                    sp_e.wait_ge(wo_l_ready, j - 1)
                load_piece((4 + j) % RAW, gate_up(0, j))
            for j in range(2):
                sp_e.wait_ge(wo_l_ready, j + 3)
                load_piece((8 + j) % RAW, gate_up(1, j))
            for t in range(TILES):
                sp_e.wait_ge(v_ready, t + 1)
                sp_e.dma_start(out_t[t], h_row[t % 2][:, :]).then_inc(h_stored[t % 2], 16)
                sp_e.dma_start(v_dram[P * t:P * (t + 1), :], v_row[:, :]).then_inc(v_stored, 16)
                if t + 2 < TILES:
                    sp_e.wait_ge(h_stored[t % 2], 16 * (t // 2 + 1))
                    sp_e.dma_start(h_row[t % 2][:, :], x_t[t + 2]).then_inc(hx[t % 2], 16)
            for j in range(2, 6):
                sp_e.wait_ge(ew_l_ready, j - 1)
                load_piece((8 + j) % RAW, gate_up(1, j) if j < 4 else down_v[0][:, PIECE * (j - 4):PIECE * (j - 3)])
            sp_e.wait_ge(table_written, 16 * 2 * TILES)
            sp_e.dma_start(table[:, :, :], table_dram.rearrange("(p b) c -> p b c", b=MAX_BLOCKS)).then_inc(table_in, 16)

            def expert_pieces(i, e, before_e):
                for j in range(6):
                    sp_e.wait_ge(ew_l_ready, 6 * i + j - 7)
                    if j < 4:
                        v = (gate_v, up_v)[j // 2]
                        src = v[bass.ds(e, 1), :, PIECE * (j % 2):PIECE * (j % 2 + 1)]
                    else:
                        src = down_v[bass.ds(before_e, 1), :, PIECE * (j - 4):PIECE * (j - 3)]
                    sp_e.dma_start(raw[(8 + j) % RAW][:, :], src.rearrange("e p n -> p (e n)")).then_inc(
                        raw_in[(8 + j) % RAW], 16)

            with sp_e.Fori(2, EXPERTS) as i:
                expert_pieces(i, i, i - 1)
            sp_e.wait_ge(addressed, 1)
            blocks = sp_e.value_load(control[0:1, 0:1], min_val=0, max_val=MAX_BLOCKS - 1 - EXPERTS) + EXPERTS
            with sp_e.If(blocks > EXPERTS):
                with sp_e.Fori(EXPERTS, blocks) as i:
                    e_now = sp_e.value_load(control[0:1, bass.ds(i - EXPERTS + 2, 1)], min_val=0, max_val=EXPERTS - 1)
                    e_old = sp_e.value_load(control[0:1, bass.ds(i - EXPERTS + 1, 1)], min_val=0, max_val=EXPERTS - 1)
                    expert_pieces(i, e_now, e_old)
            e_last = sp_e.value_load(control[0:1, bass.ds(blocks - EXPERTS + 1, 1)], min_val=0, max_val=EXPERTS - 1)
            for j in range(2):
                sp_e.wait_ge(ew_l_ready, 6 * blocks + j - 7)
                sp_e.dma_start(raw[(8 + j) % RAW][:, :],
                               down_v[bass.ds(e_last, 1), :, PIECE * j:PIECE * (j + 1)].rearrange(
                                   "e p n -> p (e n)")).then_inc(raw_in[(8 + j) % RAW], 16)
            sp_e.wait_ge(v_stored, 16 * TILES)

        @block.gpsimd
        def _(pool):
            chain = [0]

            def link(ins, last=False):
                chain[0] += 1
                ins.then_inc(psmall, 1)
                pool.wait_ge(psmall, chain[0])

            for tile, value in ((ident, 0.0), (causal_neg, 0.0), (tri_f, -1.0), (ones_neg, -1.0), (head_mean, 0.0),
                                (suffix, 0.0), (chunk_sel, 0.0), (before, 1.0), (ones_b, 1.0), (eps_col, EPS),
                                (glr_t, 1.0)):
                last = nc.gpsimd.memset(tile[:, :], value)
            last = nc.gpsimd.memset(grp_logits[:, :], NEG)
            link(last)
            for b in range(2):
                r = slice(64 * b, 64 * b + 64)
                nc.gpsimd.memset(head_mean[r, r], 1.0 / SB_DIM)
                nc.gpsimd.memset(suffix[r, r], 1.0 / TAU)
                last = nc.gpsimd.memset(chunk_sel[r, b:b + 1], 1.0 / TAU)
            link(last)

            def triangle(tile, fill, op, sign):
                return nc.gpsimd.affine_select(out=tile[:, :], in_=tile[:, :], compare_op=op, fill=fill, base=0,
                                               pattern=[[-sign, P]], channel_multiplier=sign)

            triangle(ident, 1.0, ALU.not_equal, 1)
            triangle(causal_neg, NEG, ALU.is_gt, -1)
            triangle(tri_f, 0.0, ALU.is_ge, 1)
            triangle(suffix, 0.0, ALU.is_gt, 1)
            link(triangle(before, 0.0, ALU.is_gt, -1))
            nc.gpsimd.iota(iota[:, :], pattern=[[1, EXPERTS]], base=0, channel_multiplier=0,
                           allow_small_or_imprecise_dtypes=True)
            nc.gpsimd.iota(payload[:, :, :, 0].bitcast(i32), pattern=[[P, TILES], [0, 2]], base=0,
                           channel_multiplier=1).then_inc(fixed, 1)

            for s in range(1, NU + 1):
                n, u = s - 1, units[s - 1]
                if not u["last"]:
                    pool.wait_ge(sp_done, n + 1)
                    if s == 1:
                        for i in range(3):
                            nc.gpsimd.memset(state[i][:, :, :], 0.0)
                    if n >= 3:
                        pool.wait_ge(tail_done, n - 1)
                    new, old, lo = later[n % 3], later[(n - 1) % 3], u["lo"]
                    mid = lo + P if u["diag"] else lo
                    if laters(n):
                        pool.wait_ge(later_done, laters(n))
                    if u["diag"]:
                        last = nc.gpsimd.tensor_copy(new[:, lo:mid], sp[n % 3][:, lo:mid])
                    if not u["first"]:
                        last = nc.gpsimd.tensor_tensor(new[:, mid:HALF], old[:, mid:HALF], sp[n % 3][:, mid:HALF], ADD)
                    last.then_inc(later_done, 1)
                if (s - 5) % WINDOW == 0 and s >= 5 and (s - 5) // WINDOW < TILES:
                    t = (s - 5) // WINDOW
                    pool.wait_ge(g_silu, t + 1)
                    nc.gpsimd.tensor_tensor(gsig[:, :].rearrange("p (h n) -> p h n", n=GLA_V),
                                            gsig[:, :].rearrange("p (h n) -> p h n", n=GLA_V),
                                            gla_gain[:, :].rearrange("p (a n) -> p a n", a=1).broadcast_to(
                                                [P, GLA_HEADS, GLA_V]), MUL).then_inc(g_gain, 1)

            pool.wait_ge(addressed, 1)
            pool.wait_ge(table_init, 16)
            for n in range(2 * TILES):
                pool.indirect_dma_start(out=table_dram, out_offset=bass.IndirectOffsetOnAxis(ap=address[:, n:n + 1], axis=0),
                                        in_=payload[:, n // 2, n % 2, :], in_offset=None).then_inc(table_written, 16)
            pool.wait_ge(table_in, 16)
            blocks = pool.value_load(control[0:1, 0:1], min_val=0, max_val=MAX_BLOCKS - 1 - EXPERTS) + EXPERTS
            pool.wait_ge(v_stored, 16 * TILES)
            for i in range(2):
                pool.wait_ge(h_stored[i], 16 * TILES // 2)
            pool.wait_ge(xb_clear, 1)

            def held(semaphore, value):
                value = value if isinstance(value, int) else pool.to_reg(value)
                pool.wait_ge(table_in, 16)
                pool.wait_ge(semaphore, value)

            def gather(i):
                nc.gpsimd.tensor_copy(gather_idx[:, :], table[:, bass.ds(i, 1), 0]).then_inc(idx_ready, 1)
                held(idx_ready, i + 1)
                pool.indirect_dma_start(out=xb[:, :], out_offset=None, in_=v_dram,
                                        in_offset=bass.IndirectOffsetOnAxis(ap=gather_idx[:, :], axis=0),
                                        bounds_check=T - 1, oob_is_err=False).then_inc(rows_in, 16)

            def rows(i):
                nc.gpsimd.tensor_copy(scatter_row[:, :], table[:, bass.ds(i, 1), :].rearrange("p a c -> p (a c)")).then_inc(row_ready, 1)

            def scatter(i):
                pool.indirect_dma_start(out=out_rows, out_offset=bass.IndirectOffsetOnAxis(ap=scatter_row[:, 0:1], axis=0),
                                        in_=y_row[:, :], in_offset=None, bounds_check=T - 1, oob_is_err=False,
                                        compute_op=ADD).then_inc(y_added, 16)

            gather(0)
            rows(0)
            for i in range(1, 3):
                pool.wait_ge(x_turned, i)
                gather(i)
            with pool.Fori(1, blocks - 1) as i:
                held(x_turned, i + 2)
                gather(i + 2)
                held(y_ready, i)
                scatter(i - 1)
                held(y_added, 16 * i)
                rows(i)
            for back in (2, 1):
                held(y_ready, blocks - back + 1)
                scatter(blocks - back)
                held(y_added, 16 * (blocks - back + 1))
                if back == 2:
                    rows(blocks - 1)

        @block.tensor
        def _(pe):
            mm = nc.tensor.matmul

            def three(ps, lh, ll, rh, rl, start, stop):
                mm(ps, lh, rh, start=start, stop=False)
                mm(ps, lh, rl, start=False, stop=False)
                return mm(ps, ll, rh, start=False, stop=stop)

            pe.wait_ge(fixed, 1)
            for t in range(TILES):
                pe.wait_ge(u_ready, t + 1)
                if t >= 2:
                    pe.wait_ge(uh_ready, t - 1)
                    pe.wait_ge(ul_ready, t - 1)
                rows = u_row[t % 2][:, :].rearrange("p (d k) -> p k d", k=KT)
                for k in range(KT):
                    last = nc.tensor.transpose(bank[2 * (t % 2) + k // 4][:, P * (k % 4):P * (k % 4 + 1)], rows[:, k, :],
                                               ident[:, :])
                last.then_inc(u_turned, 1)

            for n in range(2 * len(ORDER)):
                c, name = n // 2, ORDER[n // 2]
                pe.wait_ge(win_l_ready, n + 1)
                if n == 0:
                    pe.wait_ge(ul_ready, TILES)
                wh, wl = win_h[n % 2], win_l[n % 2]
                for u in range(8):
                    if n % 2 == 0 and c:
                        pe.wait_ge(unit_out, 8 * (c - 1) + u + 1)
                    for kk in range(4):
                        k = 4 * (n % 2) + kk
                        flags = dict(start=k == 0, stop=k == KT - 1)
                        if name in ("gv", "gr", "v"):
                            tok = slice(P * u, P * u + P)
                            last = three(bank[u][:, :], u_h[:, k, tok], u_l[:, k, tok], wh[:, kk, :], wl[:, kk, :], **flags)
                        else:
                            col, tok = slice(P * (u // 2), P * (u // 2) + P), slice(HALF * (u % 2), HALF * (u % 2) + HALF)
                            last = three(bank[u][:, :], wh[:, kk, col], wl[:, kk, col], u_h[:, k, tok], u_l[:, k, tok], **flags)
                    if n % 2:
                        last.then_inc(unit_done, 1)
                    elif u == 7:
                        last.then_inc(win_used, 1)
            pe.wait_ge(glr_split, 2)
            pe.wait_ge(unit_out, 8 * len(ORDER))
            for t in range(TILES):
                tok = slice(P * t, P * t + P)
                for k in range(KT):
                    last = three(bank[0][:, RANK * t:RANK * (t + 1)], u_h[:, k, tok], u_l[:, k, tok], glr_h[:, k, :],
                                 glr_l[:, k, :], start=k == 0, stop=k == KT - 1)
            last.then_inc(glr_done, 1)

            def head_norm(key):
                pe.wait_ge(sq_done, norm_order[key] + 1)
                if norm_order[key]:
                    pe.wait_ge(rs_done, norm_order[key])
                mm(bank[7][:, :], head_mean[:, :], sq[:, :], start=True, stop=True).then_inc(ms_done, 1)

            for b in range(QN):
                head_norm(("qk", 0, b))

            pe.wait_ge(consts_in, 16 * (N_CONSTS + 1))
            pe.wait_ge(glr_out, 1)
            pe.wait_ge(fixed, 2)
            for s in range(SLOT_END):
                if s < NU:
                    u = units[s]
                    row, q0 = slice(64 * (u["hd"] % 2), 64 * (u["hd"] % 2) + 64), HALF * u["qc"]
                    pe.wait_ge(q_normed, 4 * u["pair"] + 4)
                    if s >= 4:
                        pe.wait_ge(prob_done, s - 3)
                    z = bank[s % 4][:, u["lo"]:HALF]
                    last = mm(z, k_t[row, u["pair"], P * u["j"]:P * u["j"] + P],
                              q_t[row, u["pair"], q0 + u["lo"]:q0 + HALF], start=True, stop=True)
                    if u["diag"]:
                        last = mm(bank[s % 4][:, u["lo"]:u["lo"] + P], ident_b[:, :], causal_neg[:, :], start=False,
                                  stop=True, skip_group_check=True)
                    last.then_inc(qk_done, 1)
                if 2 <= s and s - 2 < NU:
                    n, u = s - 2, units[s - 2]
                    z = bank[n % 4][:, u["lo"]:HALF]
                    pe.wait_ge(spl_done, n + 1)
                    mm(z, tri_neg[:, :], sp_h[n % 3][:, u["lo"]:HALF], start=False, stop=True, skip_group_check=True)
                    last = mm(z, tri_neg[:, :], sp_l[n % 3][:, u["lo"]:HALF], start=False, stop=True,
                              skip_group_check=True)
                    mid = u["lo"] + P if u["diag"] else u["lo"]
                    if not u["first"]:
                        pe.wait_ge(later_done, laters(n))
                        last = mm(bank[n % 4][:, mid:HALF], ones_neg[:, :], later[(n - 1) % 3][:, mid:HALF], start=False,
                                  stop=True, skip_group_check=True)
                    last.then_inc(tail_done, 1)
                if 3 <= s and s - 3 < NU:
                    n, u = s - 3, units[s - 3]
                    pe.wait_ge(prob_done, n + 1)
                    half = slice(64 * (u["hd"] % 2), 64 * (u["hd"] % 2) + 64)
                    g = 2 * u["pair"] + (u["qc"] == 0)
                    if u["first"] and g:
                        pe.wait_ge(sq_done, norm_order[("o", g - 1)] + 1)
                    mm(bank[4][half, u["lo"]:HALF], v_s[:, u["j"], SB_DIM * u["hd"]:SB_DIM * (u["hd"] + 1)],
                       prob[n % 2][:, u["lo"]:HALF], start=u["first"], stop=u["last"],
                       skip_group_check=True).then_inc(pv_done, 1)
                if s >= 5 and s - 5 in GROUP_END:
                    head_norm(("o", GROUP_END[s - 5]))
                if s >= 1 and norm_event(s - 1):
                    head_norm(("qk", *norm_event(s - 1)))
                t, r = divmod(s, WINDOW)
                if t < TILES and r == 0:
                    if t:
                        pe.wait_ge(g_state, 2 * t)
                    for p in range(2):
                        nc.tensor.transpose(bank[6][:, P * p:P * p + P], gk_t[:, p, P * t:P * t + P], ident[:, :])
                    nc.tensor.transpose(bank[6][0:RANK, 256:256 + P], glr[:, t, :], ident[:, :]).then_inc(g_turned, 1)
                if t < TILES and r == 2:
                    pe.wait_ge(g_turned_out, t + 1)
                    mm(bank[6][:, 0:256], glr_t[:, :], gate_w2[:, :], start=True, stop=True).then_inc(g_logit, 1)
                if t < TILES and r == 5:
                    pe.wait_ge(g_log, t + 1)
                    mm(bank[6][:, 0:256], suffix[:, :], log_g[:, :], start=True, stop=True)
                    for p in range(2):
                        last = mm(bank[6][:, 256 + 2 * p:258 + 2 * p], log_g[:, P * p:P * p + P], chunk_sel[:, :],
                                  start=True, stop=True)
                    last.then_inc(g_decay, 1)
                for c, slot in ((0, 7), (1, 9)):
                    if t < TILES and r == slot:
                        if c == 0:
                            pe.wait_ge(g_kdec, t + 1)
                            pe.wait_ge(gvr_in, 32 * (t + 1))
                        else:
                            pe.wait_ge(g_state, 2 * t + 1)
                        tok = slice(CHUNK * c, CHUNK * c + CHUNK)
                        for p in range(2):
                            last = mm(bank[6][:, 256 * p:256 * p + 256], k_dec[tok, P * p:P * p + P],
                                      gv_s[tok, 256 * p:256 * p + 256], start=True, stop=True)
                        last.then_inc(g_kv, 1)
                for c, slot in ((0, 9), (1, 11)):
                    if t < TILES and r == slot:
                        n = 2 * t + c
                        pe.wait_ge(g_state, n + 1)
                        if c == 0 and t:
                            pe.wait_ge(g_mixl, t)
                            pe.wait_ge(g_mixh, t)
                        for p in range(2):
                            last = mm(bank[5][64 * c:64 * c + 64, 256 * p:256 * p + 256],
                                      gq_t[:, p, CHUNK * n:CHUNK * n + CHUNK], state[n % 3][:, p, :], start=True, stop=True)
                        last.then_inc(g_o, 1)
                if t >= 1 and r == 3 and t <= TILES:
                    pe.wait_ge(g_go, t)
                    for p in range(GLA_HEADS):
                        last = nc.tensor.transpose(bank[5][:, P * p:P * p + P], go[:, P * p:P * p + P], ident[:, :])
                    last.then_inc(g_got, 1)

            pe.wait_ge(mix_ready, 8)
            pe.wait_ge(g_mixh, TILES)
            pe.wait_ge(g_mixl, TILES)
            for t in range(TILES + 2):
                if t < TILES:
                    tok = slice(P * t, P * t + P)
                    if t >= 2:
                        pe.wait_ge(h_ready, t - 1)
                    for k in range(KT):
                        if t == 0 and k % 2 == 0:
                            pe.wait_ge(wo_l_ready, k // 2 + 1)
                        for half in range(2):
                            col = slice(HALF * half, HALF * half + HALF)
                            last = three(bank[2 * (t % 2) + half][:, :], mix_h[:, k, tok], mix_l[:, k, tok],
                                         wo_h[:, k, col], wo_l[:, k, col], start=k == 0, stop=k == KT - 1)
                    last.then_inc(wo_done, 1)
                if 1 <= t <= TILES:
                    pe.wait_ge(v_ready, t)
                    if t >= 2:
                        pe.wait_ge(vt_ready, t - 1)
                    rows = v_row[:, :].rearrange("p (d k) -> p k d", k=KT)
                    for k in range(KT):
                        last = nc.tensor.transpose(bank[4 + k // 4][:, P * (k % 4):P * (k % 4 + 1)], rows[:, k, :],
                                                   ident[:, :])
                    last.then_inc(v_turned, 1)
                if t >= 2:
                    pe.wait_ge(vt_ready, t - 1)
                    if t >= 3:
                        pe.wait_ge(logit_out, t - 2)
                    for k in range(KT):
                        last = mm(bank[6][:, 0:LOGITS], v_t[:, k, :], router_w[:, k, :], start=k == 0, stop=k == KT - 1)
                    last.then_inc(logit_done, 1)
            pe.wait_ge(routed, TILES)
            for t in range(TILES):
                for b in range(t + 1):
                    mm(bank[7][:, EXPERTS * t:EXPERTS * (t + 1)], (before if b == t else ones_b)[:, :], chosen_any[:, b, :],
                       start=b == 0, stop=b == t)
            for b in range(TILES):
                last = mm(bank[7][:, EXPERTS * TILES:EXPERTS * (TILES + 1)], ones_b[:, :], chosen_any[:, b, :],
                          start=b == 0, stop=b == TILES - 1)
            last.then_inc(ranked, 1)

            def turn_rows(i):
                pe.wait_ge(rows_in, 16 * (i + 1))
                rows = xb[:, :].rearrange("p (d k) -> p k d", k=KT)
                for k in range(KT):
                    last = nc.tensor.transpose(bank[2 + k // 4][:, P * (k % 4):P * (k % 4 + 1)], rows[:, k, :], ident[:, :])
                last.then_inc(x_turned, 1)

            def gate_up(i, m0):
                count, slot0 = m0
                pe.wait_ge(xh_ready, i + 1)
                pe.wait_ge(xl_ready, i + 1)
                for j in range(4):
                    pe.wait_ge(ew_l_ready, count + j + 1)
                    wh = ew_h[(slot0 + j) % SPLIT][:, :].rearrange("p (k n) -> p k n", n=FF)
                    wl = ew_l[(slot0 + j) % SPLIT][:, :].rearrange("p (k n) -> p k n", n=FF)
                    for kk in range(4):
                        k = 4 * (j % 2) + kk
                        last = three(bank[j // 2][:, :], xb_h[:, k, :], xb_l[:, k, :], wh[:, kk, :], wl[:, kk, :],
                                     start=k == 0, stop=k == KT - 1)
                    last.then_inc(ew_used, 1)

            def turn_act(i):
                pe.wait_ge(act_done, i + 1)
                rows = act_row[:, :].rearrange("p (f k) -> p k f", k=FT)
                for k in range(FT):
                    last = nc.tensor.transpose(bank[4][:, P * k:P * k + P], rows[:, k, :], ident[:, :])
                last.then_inc(a_turned, 1)

            def down(i, m0, first=False):
                count, slot0 = m0
                pe.wait_ge(ah_ready, i + 1)
                pe.wait_ge(al_ready, i + 1)
                if not first:
                    pe.wait_ge(y_ready, i)
                for j in range(2):
                    pe.wait_ge(ew_l_ready, count + j + 1)
                    wh = ew_h[(slot0 + j) % SPLIT][:, :].rearrange("p (k n) -> p k n", n=D)
                    wl = ew_l[(slot0 + j) % SPLIT][:, :].rearrange("p (k n) -> p k n", n=D)
                    for kk in range(2):
                        k = 2 * j + kk
                        for half in range(2):
                            col = slice(HALF * half, HALF * half + HALF)
                            last = three(bank[5 + half][:, :], a_h[:, k, :], a_l[:, k, :], wh[:, kk, col], wl[:, kk, col],
                                         start=k == 0, stop=k == FT - 1)
                    last.then_inc(ew_used, 1)

            pe.wait_ge(addressed, 1)
            blocks = pe.value_load(control[0:1, 0:1], min_val=0, max_val=MAX_BLOCKS - 1 - EXPERTS) + EXPERTS
            turn_rows(0)
            gate_up(0, (0, 0))
            turn_rows(1)
            turn_act(0)
            gate_up(1, (4, 4))
            turn_rows(2)
            down(0, (8, 2), first=True)
            turn_act(1)
            with pe.Fori(2, blocks) as i:
                gate_up(i, (6 * i - 2, 4))
                turn_rows(i + 1)
                down(i - 1, (6 * i + 2, 2))
                turn_act(i)
            down(blocks - 1, (6 * blocks - 2, 4))

        @block.scalar
        def _(act):
            chain = [0]

            def link(ins):
                chain[0] += 1
                ins.then_inc(asmall, 1)
                act.wait_ge(asmall, chain[0])

            A = nc.scalar.activation
            nc.scalar.preload_act_table_set("natural_log_exp_and_others")

            def rstd_of(dst, src, ln_bias=None):
                link(A(dst, src, ACT.Ln, bias=ln_bias) if ln_bias is not None else A(dst, src, ACT.Ln))
                return A(dst, dst, ACT.Exp, scale=-0.5)

            def split_win(n):
                act.wait_ge(win_in[n % 2], 16 * (n // 2 + 1))
                if n >= 2:
                    if n % 2 == 0:
                        act.wait_ge(win_used, n // 2)
                    else:
                        act.wait_ge(unit_done, 8 * (n // 2))
                A(win_h[n % 2][:, :, :].rearrange("p k n -> p (k n)"), win_raw[n % 2][:, :], ACT.Copy).then_inc(win_h_ready, 1)

            def u_high(t):
                act.wait_ge(u_turned, t + 1)
                for b in range(2):
                    last = A(u_h[:, 4 * b:4 * b + 4, P * t:P * t + P],
                             bank[2 * (t % 2) + b][:, :].rearrange("p (k n) -> p k n", n=P), ACT.Copy)
                last.then_inc(uh_ready, 1)

            for t in range(TILES):
                act.wait_ge(xs[t], 16)
                A(squares[:, :], x_in[t][:, :], ACT.Square, accum_out=stat[:, 0:1]).then_inc(square_done, 1)
                act.wait_ge(mean_done, t + 1)
                rstd_of(stat[:, 2:3], stat[:, 1:2]).then_inc(rstd_done, 1)
                if t:
                    u_high(t - 1)
            split_win(0)
            u_high(TILES - 1)
            split_win(1)
            n_spill = 0
            for c, name in enumerate(ORDER):
                if 2 * c + 2 < 2 * len(ORDER):
                    split_win(2 * c + 2)
                else:
                    act.wait_ge(glr_in, 16)
                    A(glr_h[:, :, :], glr_raw[:, :, :], ACT.Copy).then_inc(glr_split, 1)
                for u in range(8):
                    act.wait_ge(unit_done, 8 * c + u + 1)
                    src = bank[u][:, :]
                    if name in ("gv", "gr"):
                        slot = n_spill % 2
                        if n_spill >= 2:
                            act.wait_ge(spilled[slot], 16 * (n_spill // 2))
                        A(spill[slot][:, :], src, ACT.Copy).then_inc(unit_out, 1)
                        act.wait_ge(unit_out, 8 * c + u + 1)
                        act.dma_start((gv_dram if name == "gv" else gr_dram)[u], spill[slot][:, :]).then_inc(spilled[slot], 16)
                        n_spill += 1
                    elif name == "v":
                        A(v_s[:, u, :], src, ACT.Copy).then_inc(unit_out, 1)
                    else:
                        g, tok = u // 2, slice(HALF * (u % 2), HALF * (u % 2) + HALF)
                        if name == "gqk":
                            A((gq_t if g < 2 else gk_t)[:, g % 2, tok], src, ACT.Copy,
                              scale=GLA_K ** -0.5 if g < 2 else 1.0).then_inc(unit_out, 1)
                        else:
                            A((q_t if name == "q" else k_t)[:, g, tok], src, ACT.Copy).then_inc(unit_out, 1)
                if 2 * c + 3 < 2 * len(ORDER):
                    split_win(2 * c + 3)
            act.wait_ge(glr_done, 1)
            A(glr[:, :, :].rearrange("p t n -> p (t n)"), bank[0][:, 0:RANK * TILES], ACT.Copy).then_inc(glr_out, 1)

            def norm_square(key):
                n = norm_order[key]
                if n:
                    act.wait_ge(ms_done, n)
                if key[0] == "qk":
                    A(sq[:, :], qk_block(key[2], key[1]), ACT.Square).then_inc(sq_done, 1)
                else:
                    g = key[1]
                    if g:
                        act.wait_ge(mix_ready, g)
                    A(sq[:, :], bank[4][:, :], ACT.Square)
                    A(o_s[:, :], bank[4][:, :], ACT.Copy).then_inc(sq_done, 1)

            def norm_rstd(key):
                n = norm_order[key]
                act.wait_ge(ms_done, n + 1)
                if n:
                    act.wait_ge(q_normed, before_norm[key][0])
                    act.wait_ge(mix_ready, before_norm[key][1]) if before_norm[key][1] else None
                link(A(rs[:, :], bank[7][:, :], ACT.Ln, bias=eps_col[:, :]))
                A(rs[:, :], rs[:, :], ACT.Exp, scale=-0.5).then_inc(rs_done, 1)

            before_norm = {}
            seen = [0, 0]
            for key in sorted(norm_order, key=norm_order.get):
                before_norm[key] = tuple(seen)
                seen[0 if key[0] == "qk" else 1] += 1

            act.wait_ge(fixed, 1)
            for b in range(QN):
                norm_square(("qk", 0, b))
                norm_rstd(("qk", 0, b))

            for s in range(SLOT_END):
                if s >= 4 and s - 4 in GROUP_END:
                    act.wait_ge(pv_done, s - 3)
                    norm_square(("o", GROUP_END[s - 4]))
                if s < NU:
                    u = units[s]
                    w = soft[s % 2][:, u["lo"]:HALF]
                    act.wait_ge(cap_done, s + 1)
                    link(A(w, w, ACT.Exp))
                    A(w, w, ACT.Ln, bias=1.0).then_inc(ln_done, 1)
                if 2 <= s and s - 2 < NU:
                    n, u = s - 2, units[s - 2]
                    act.wait_ge(tail_done, n + 1)
                    if n >= 2:
                        act.wait_ge(pv_done, n - 1)
                    A(prob[n % 2][:, u["lo"]:HALF], bank[n % 4][:, u["lo"]:HALF], ACT.Exp).then_inc(prob_done, 1)
                if s >= 6 and s - 6 in GROUP_END:
                    norm_rstd(("o", GROUP_END[s - 6]))
                if norm_event(s):
                    norm_square(("qk", *norm_event(s)))
                if s >= 2 and norm_event(s - 2):
                    norm_rstd(("qk", *norm_event(s - 2)))
                t, r = divmod(s, WINDOW)
                if t < TILES and r == 1:
                    act.wait_ge(g_turned, t + 1)
                    if t:
                        act.wait_ge(g_kdec, t)
                    A(gk_s[:, :], bank[6][:, 0:256], ACT.Copy)
                    A(glr_t[0:RANK, :], bank[6][0:RANK, 256:256 + P], ACT.Copy).then_inc(g_turned_out, 1)
                if t < TILES and r == 3:
                    act.wait_ge(g_rcap, t + 1)
                    link(A(gsig[:, :], gsig[:, :], ACT.Exp, scale=-1.0))
                    link(A(gsig[:, :], gsig[:, :], ACT.Ln, bias=1.0))
                    A(gsig[:, :], gsig[:, :], ACT.Exp, scale=-1.0).then_inc(g_sig, 1)
                    act.wait_ge(g_cap, t + 1)
                    link(A(log_g[:, :], log_g[:, :], ACT.Exp, scale=-1.0))
                    A(log_g[:, :], log_g[:, :], ACT.Ln, bias=1.0).then_inc(g_ln, 1)
                if t < TILES and r == 6:
                    act.wait_ge(g_decay, t + 1)
                    A(k_dec[:, :], bank[6][:, 0:256], ACT.Exp)
                    A(gstat[:, 0:4], bank[6][:, 256:260], ACT.Exp).then_inc(g_exp, 1)
                if 1 <= t <= TILES and r == 0:
                    act.wait_ge(g_o, 2 * t)
                    if t >= 2:
                        act.wait_ge(g_got, t - 1)
                    A(go[:, :], bank[5][:, :], ACT.Square).then_inc(g_sq, 1)
                if 1 <= t <= TILES and r == 1:
                    act.wait_ge(g_ms, t)
                    rstd_of(gstat[:, 8:12], gstat[:, 12:16]).then_inc(g_rs, 1)
                if 1 <= t <= TILES and r == 4:
                    act.wait_ge(g_got, t)
                    A(mix_h[:, 4:8, P * (t - 1):P * t], bank[5][:, :].rearrange("p (k n) -> p k n", n=P),
                      ACT.Copy).then_inc(g_mixh, 1)

            act.wait_ge(pv_done, NU)
            act.wait_ge(g_o, 2 * TILES)
            for n in range(4):
                act.wait_ge(raw_in[n], 16)
                A(wo_h[:, 2 * n:2 * n + 2, :].rearrange("p k n -> p (k n)"), raw[n][:, :], ACT.Copy).then_inc(wo_h_ready, 1)
            for t in range(TILES + 2):
                if t < TILES:
                    act.wait_ge(h_ready, t + 1)
                    if t:
                        act.wait_ge(v_turned, t)
                        act.wait_ge(v_stored, 16 * t)
                    A(v_row[:, :], h_row[t % 2][:, :], ACT.Square, accum_out=stat[:, 3:4]).then_inc(h_square, 1)
                    act.wait_ge(h_mean, t + 1)
                    rstd_of(stat[:, 5:6], stat[:, 4:5]).then_inc(h_rstd, 1)
                if 1 <= t <= TILES:
                    act.wait_ge(v_turned, t)
                    if t >= 2:
                        act.wait_ge(logit_done, t - 1)
                    for b in range(2):
                        last = A(v_t[:, 4 * b:4 * b + 4, :], bank[4 + b][:, :].rearrange("p (k n) -> p k n", n=P), ACT.Copy)
                    last.then_inc(vt_ready, 1)
                if t >= 2:
                    act.wait_ge(r_max, t - 1)
                    A(r_small[:, 0:N_GROUPS], grp_logits[:, 0:N_GROUPS], ACT.Exp, bias=stat[:, 6:7],
                      accum_out=stat[:, 7:8]).then_inc(r_exp, 1)
                    act.wait_ge(r_diff, t - 1)
                    A(stat[:, 9:10], stat[:, 8:9], ACT.Exp).then_inc(r_ratio, 1)

            def high(count, slot, raw_slot, uses, guard=True):
                act.wait_ge(raw_in[raw_slot], 16 * uses)
                if guard:
                    act.wait_ge(ew_used, count - SPLIT + 1)
                A(ew_h[slot % SPLIT][:, :], raw[raw_slot][:, :], ACT.Copy).then_inc(ew_h_ready, 1)

            def x_high(i):
                act.wait_ge(x_turned, i + 1)
                for b in range(2):
                    last = A(xb_h[:, 4 * b:4 * b + 4, :], bank[2 + b][:, :].rearrange("p (k n) -> p k n", n=P), ACT.Copy)
                last.then_inc(xh_ready, 1)

            def silu_of(i):
                act.wait_ge(gate_or_up(i, 2)[0], gate_or_up(i, 2)[1])
                A(silu[:, :], bank[0][:, :], ACT.Silu).then_inc(silu_done, 1)

            def gate_or_up(i, j):
                return ew_used, used_before(i) + j

            def used_before(i):
                return 0 if isinstance(i, int) and i == 0 else (4 if isinstance(i, int) and i == 1 else 6 * i - 2)

            def back(i):
                act.wait_ge(down_count, down_value(i))
                act.wait_ge(row_ready, i + 1)
                for b in range(2):
                    last = A(y_row[:, HALF * b:HALF * b + HALF], bank[5 + b][:, :], ACT.Copy,
                             scale=scatter_row[:, 1:2].bitcast(fp32))
                last.then_inc(y_ready, 1)

            down_count = ew_used

            def down_value(i):
                return 6 * i + 10

            def a_high(i):
                act.wait_ge(a_turned, i + 1)
                A(a_h[:, :, :], bank[4][:, :].rearrange("p (k n) -> p k n", n=P), ACT.Copy).then_inc(ah_ready, 1)

            act.wait_ge(wo_done, TILES)
            for m in range(4):
                high(m, m, (4 + m) % RAW, (4 + m) // RAW + 1, guard=False)
            act.wait_ge(addressed, 1)
            blocks = act.value_load(control[0:1, 0:1], min_val=0, max_val=MAX_BLOCKS - 1 - EXPERTS) + EXPERTS
            x_high(0)
            for j in range(4):
                high(4 + j, 4 + j, (8 + j) % RAW, (8 + j) // RAW + 1, guard=4 + j >= SPLIT)
                if j == 1:
                    silu_of(0)
            x_high(1)
            for j in range(4, 6):
                high(4 + j, 4 + j, (8 + j) % RAW, (8 + j) // RAW + 1)
            a_high(0)

            def step(i, last=False):
                if not last:
                    for j in range(2):
                        high(6 * i + 4 + j, 4 + j, (8 + j) % RAW, i + (8 + j) // RAW + 1)
                silu_of(i)
                if not last:
                    for j in range(2, 4):
                        high(6 * i + 4 + j, 4 + j, (8 + j) % RAW, i + (8 + j) // RAW + 1)
                x_high(i + 1)
                for j in range(4, 6):
                    if last:
                        high(6 * i + j, j, (4 + j) % RAW, i + (4 + j) // RAW + 1)
                    else:
                        high(6 * i + 4 + j, 4 + j, (8 + j) % RAW, i + (8 + j) // RAW + 1)
                back(i - 1)
                a_high(i)

            step(1)
            with act.Fori(2, blocks - 1) as i:
                step(i)
            step(blocks - 1, last=True)
            act.wait_ge(ew_used, 6 * blocks)
            act.wait_ge(row_ready, blocks)
            for b in range(2):
                last = A(y_row[:, HALF * b:HALF * b + HALF], bank[5 + b][:, :], ACT.Copy,
                         scale=scatter_row[:, 1:2].bitcast(fp32))
            last.then_inc(y_ready, 1)

        @block.vector
        def _(dve):
            V = nc.vector
            chain = [0]

            def link(ins):
                chain[0] += 1
                ins.then_inc(small, 1)
                dve.wait_ge(small, chain[0])

            def low(dst, src, high):
                return V.tensor_tensor(dst, src, high.bitcast(fp32), SUB)

            link(V.memset(table_fill[:, :], 0))
            V.memset(table_fill[:, :].rearrange("p (b c) -> p b c", c=2)[:, :, 0], T).then_inc(fill_ready, 1)
            dve.wait_ge(fixed, 1)
            V.tensor_copy(ident_b[:, :], ident[:, :])
            V.tensor_copy(tri_neg[:, :], tri_f[:, :]).then_inc(fixed, 1)

            def u_low(t):
                dve.wait_ge(uh_ready, t + 1)
                for b in range(2):
                    dst = (slice(None), slice(4 * b, 4 * b + 4), slice(P * t, P * t + P))
                    last = low(u_l[dst], bank[2 * (t % 2) + b][:, :].rearrange("p (k n) -> p k n", n=P), u_h[dst])
                last.then_inc(ul_ready, 1)

            dve.wait_ge(gain_in, 16)
            for t in range(TILES):
                dve.wait_ge(square_done, t + 1)
                V.tensor_scalar(stat[:, 1:2], stat[:, 0:1], 1.0 / D, EPS, MUL, ADD).then_inc(mean_done, 1)
                dve.wait_ge(rstd_done, t + 1)
                if t >= 2:
                    dve.wait_ge(u_turned, t - 1)
                V.scalar_tensor_tensor(out=u_row[t % 2][:, :], in0=x_in[t][:, :], scalar=stat[:, 2:3], in1=gain1[:, :],
                                       op0=MUL, op1=MUL).then_inc(u_ready, 1)
                if t:
                    u_low(t - 1)

            def win_low(n):
                dve.wait_ge(win_h_ready, n + 1)
                low(win_l[n % 2][:, :, :].rearrange("p k n -> p (k n)"), win_raw[n % 2][:, :],
                    win_h[n % 2][:, :, :].rearrange("p k n -> p (k n)")).then_inc(win_l_ready, 1)

            win_low(0)
            u_low(TILES - 1)
            for n in range(1, 2 * len(ORDER)):
                win_low(n)
            dve.wait_ge(glr_split, 1)
            low(glr_l[:, :, :], glr_raw[:, :, :], glr_h[:, :, :]).then_inc(glr_split, 1)
            dve.wait_ge(consts_in, 16 * (N_CONSTS + 1))
            link(V.tensor_scalar(q_gain[:, :], q_gain[:, :], SB_DIM ** -0.5, None, MUL))

            def norm_qk(pair, b):
                dve.wait_ge(rs_done, norm_order[("qk", pair, b)] + 1)
                blk_ap = qk_block(b, pair)
                V.scalar_tensor_tensor(out=blk_ap, in0=blk_ap, scalar=(q_gain if b < 2 else k_gain)[:, :], in1=rs[:, :],
                                       op0=MUL, op1=MUL).then_inc(q_normed, 1)

            for b in range(QN):
                norm_qk(0, b)

            for s in range(SLOT_END):
                if s < NU:
                    u = units[s]
                    dve.wait_ge(qk_done, s + 1)
                    V.tensor_scalar(soft[s % 2][:, u["lo"]:HALF], bank[s % 4][:, u["lo"]:HALF], CAP, None,
                                    ALU.min).then_inc(cap_done, 1)
                if 1 <= s <= NU:
                    n, u = s - 1, units[s - 1]
                    cols = slice(u["lo"], HALF)
                    dve.wait_ge(ln_done, n + 1)
                    if n >= 3:
                        dve.wait_ge(later_done, laters(n - 2))
                    V.tensor_tensor(sp[n % 3][:, cols], bank[n % 4][:, cols], soft[n % 2][:, cols],
                                    ALU.max).then_inc(sp_done, 1)
                    dve.wait_ge(sp_done, n + 1)
                    if n >= 3:
                        dve.wait_ge(tail_done, n - 2)
                    link(V.tensor_copy(sp_h[n % 3][:, cols], sp[n % 3][:, cols]))
                    low(sp_l[n % 3][:, cols], sp[n % 3][:, cols], sp_h[n % 3][:, cols]).then_inc(spl_done, 1)
                if s >= 7 and s - 7 in GROUP_END:
                    g = GROUP_END[s - 7]
                    pair, q0 = g // 2, HALF * (1 - g % 2)
                    dve.wait_ge(rs_done, norm_order[("o", g)] + 1)
                    link(V.scalar_tensor_tensor(out=o_s[:, :], in0=o_s[:, :], scalar=o_gain[:, pair:pair + 1], in1=rs[:, :],
                                                op0=MUL, op1=MUL))
                    dst = (slice(None), pair, slice(q0, q0 + HALF))
                    link(V.tensor_copy(mix_h[dst], o_s[:, :]))
                    low(mix_l[dst], o_s[:, :], mix_h[dst]).then_inc(mix_ready, 1)
                if s >= 3 and norm_event(s - 3):
                    norm_qk(*norm_event(s - 3))
                t, r = divmod(s, WINDOW)
                if 1 <= t <= TILES and r == 0:
                    dve.wait_ge(g_sq, t)
                    link(V.reduce_sum(gstat[:, 4:8], go[:, :].rearrange("p (h n) -> p h n", n=GLA_V), axis=AX.X))
                    V.tensor_scalar(gstat[:, 12:16], gstat[:, 4:8], 1.0 / GLA_V, EPS, MUL, ADD).then_inc(g_ms, 1)
                if 1 <= t <= TILES and r == 2:
                    dve.wait_ge(g_rs, t)
                    dve.wait_ge(g_gain, t)
                    for h in range(GLA_HEADS):
                        c = slice(GLA_V * h, GLA_V * (h + 1))
                        last = V.scalar_tensor_tensor(out=go[:, c], in0=bank[5][:, c], scalar=gstat[:, 8 + h:9 + h],
                                                      in1=gsig[:, c], op0=MUL, op1=MUL)
                    last.then_inc(g_go, 1)
                if t < TILES and r == 2:
                    if t:
                        dve.wait_ge(g_go, t)
                    dve.wait_ge(gvr_in, 32 * (t + 1))
                    V.tensor_scalar(gsig[:, :], gr_s[:, :], -GUARD, None, ALU.max).then_inc(g_rcap, 1)
                if t < TILES and r == 3:
                    dve.wait_ge(g_logit, t + 1)
                    if t:
                        dve.wait_ge(g_decay, t)
                    V.tensor_scalar(log_g[:, :], bank[6][:, 0:256], -CAP, None, ALU.max).then_inc(g_cap, 1)
                if t < TILES and r == 4:
                    dve.wait_ge(g_sig, t + 1)
                    V.tensor_tensor(gsig[:, :], gsig[:, :], gr_s[:, :], MUL).then_inc(g_silu, 1)
                if t < TILES and r == 4:
                    dve.wait_ge(g_ln, t + 1)
                    V.scalar_tensor_tensor(out=log_g[:, :], in0=log_g[:, :], scalar=-1.0, in1=bank[6][:, 0:256],
                                           op0=MUL, op1=ALU.min).then_inc(g_log, 1)
                if t < TILES and r == 6:
                    dve.wait_ge(g_exp, t + 1)
                    V.tensor_tensor(k_dec[:, :], k_dec[:, :], gk_s[:, :], MUL).then_inc(g_kdec, 1)
                for c, slot in ((0, 8), (1, 10)):
                    if t < TILES and r == slot:
                        n = 2 * t + c
                        dve.wait_ge(g_kv, n + 1)
                        if n >= 3:
                            dve.wait_ge(g_o, n - 2)
                        for p in range(2):
                            for h in range(2):
                                row, col = slice(64 * h, 64 * h + 64), slice(GLA_V * h, GLA_V * (h + 1))
                                last = V.scalar_tensor_tensor(
                                    out=state[n % 3][row, p, col], in0=state[(n - 1) % 3][row, p, col],
                                    scalar=gstat[row, 2 * p + c:2 * p + c + 1],
                                    in1=bank[6][row, 256 * p + GLA_V * h:256 * p + GLA_V * (h + 1)], op0=MUL, op1=ADD)
                        last.then_inc(g_state, 1)
                        dve.wait_ge(g_state, n + 1)
                if 1 <= t <= TILES and r == 4:
                    dve.wait_ge(g_mixh, t)
                    dst = (slice(None), slice(4, 8), slice(P * (t - 1), P * t))
                    low(mix_l[dst], bank[5][:, :].rearrange("p (k n) -> p k n", n=P), mix_h[dst]).then_inc(g_mixl, 1)

            for n in range(4):
                dve.wait_ge(wo_h_ready, n + 1)
                cols = (slice(None), slice(2 * n, 2 * n + 2), slice(None))
                low(wo_l[cols].rearrange("p k n -> p (k n)"), raw[n][:, :], wo_h[cols].rearrange("p k n -> p (k n)")).then_inc(
                    wo_l_ready, 1)
            dve.wait_ge(gain2_in, 16)
            for t in range(TILES + 2):
                if t < TILES:
                    dve.wait_ge(wo_done, t + 1)
                    dve.wait_ge(hx[t % 2], 16 * (t // 2 + 1))
                    for b in range(2):
                        c = slice(HALF * b, HALF * b + HALF)
                        last = V.tensor_tensor(h_row[t % 2][:, c], h_row[t % 2][:, c], bank[2 * (t % 2) + b][:, :], ADD)
                    last.then_inc(h_ready, 1)
                    dve.wait_ge(h_square, t + 1)
                    V.tensor_scalar(stat[:, 4:5], stat[:, 3:4], 1.0 / D, EPS, MUL, ADD).then_inc(h_mean, 1)
                    dve.wait_ge(h_rstd, t + 1)
                    V.scalar_tensor_tensor(out=v_row[:, :], in0=h_row[t % 2][:, :], scalar=stat[:, 5:6], in1=gain2[:, :],
                                           op0=MUL, op1=MUL).then_inc(v_ready, 1)
                if t >= 2:
                    n = t - 2
                    dve.wait_ge(logit_done, n + 1)
                    V.tensor_tensor(grp_logits[:, 0:N_GROUPS], bank[6][:, 0:N_GROUPS], router_bias[:, 0:N_GROUPS], ADD)
                    last = V.tensor_tensor(exp_logits[:, :], bank[6][:, N_GROUPS:LOGITS], router_bias[:, N_GROUPS:LOGITS], ADD)
                    last.then_inc(logit_out, 1)
                    dve.wait_ge(logit_out, n + 1)
                    link(V.max(top_val[:, 0, :], grp_logits[:, :]))
                    link(V.max_index(top_idx[:, 0, :], top_val[:, 0, :], grp_logits[:, :]))
                    V.tensor_scalar(stat[:, 6:7], top_val[:, 0, 0:1], -1.0, None, MUL).then_inc(r_max, 1)
                    link(V.tensor_copy(r_small[:, 8:9], top_idx[:, 0, 0:1]))
                    link(V.tensor_scalar(r_small[:, 12:16], iota[:, 0:N_GROUPS], r_small[:, 8:9], None, ALU.is_equal))
                    link(V.tensor_tensor(masked[:, :].rearrange("p (e g) -> p e g", g=N_GROUPS),
                                         exp_logits[:, :].rearrange("p (g e) -> p e g", g=N_GROUPS),
                                         r_small[:, 12:16].rearrange("p (a g) -> p a g", a=1).broadcast_to(
                                             [P, PER_GROUP, N_GROUPS]), MUL))
                    link(V.reduce_sum(sel_logits[:, :], masked[:, :].rearrange("p (e g) -> p e g", g=N_GROUPS), axis=AX.X))
                    link(V.max(top_val[:, 1, :], sel_logits[:, :]))
                    link(V.max_index(top_idx[:, 1, :], top_val[:, 1, :], sel_logits[:, :]))
                    V.tensor_tensor(stat[:, 8:9], top_val[:, 1, 1:2], top_val[:, 1, 0:1], SUB).then_inc(r_diff, 1)
                    link(V.tensor_copy(r_small[:, 16:18], top_idx[:, 1, 0:2]))
                    link(V.scalar_tensor_tensor(out=expert_of[:, n, :], in0=r_small[:, 8:9].broadcast_to([P, 2]),
                                                scalar=float(PER_GROUP), in1=r_small[:, 16:18], op0=MUL, op1=ADD))
                    for j in range(2):
                        last = V.tensor_scalar(chosen[:, n, j, :], iota[:, :], expert_of[:, n, j:j + 1], None, ALU.is_equal)
                    link(last)
                    link(V.tensor_tensor(chosen_any[:, n, :], chosen[:, n, 0, :], chosen[:, n, 1, :], ADD))
                    dve.wait_ge(r_exp, n + 1)
                    dve.wait_ge(r_ratio, n + 1)
                    link(V.scalar_tensor_tensor(out=stat[:, 10:11], in0=stat[:, 9:10], scalar=1.0, in1=stat[:, 7:8],
                                                op0=ADD, op1=MUL))
                    link(V.reciprocal(stat[:, 11:12], stat[:, 10:11]))
                    gates = payload[:, n, :, 1].bitcast(fp32)
                    V.tensor_copy(gates[:, 0:1], stat[:, 11:12])
                    V.tensor_tensor(gates[:, 1:2], stat[:, 11:12], stat[:, 9:10], MUL).then_inc(routed, 1)
                    dve.wait_ge(routed, n + 1)

            dve.wait_ge(ranked, 1)
            counts = bank[7][:, EXPERTS * TILES:EXPERTS * (TILES + 1)]
            link(V.tensor_scalar(n_extra[:, :], counts, float(P), None, ALU.is_gt))
            for m in range(2, TILES):
                link(V.scalar_tensor_tensor(out=n_extra[:, :], in0=counts, scalar=float(P * m), in1=n_extra[:, :],
                                            op0=ALU.is_gt, op1=ADD))
            link(V.memset(big[:, 0:EXPERTS], 0.0))
            link(V.tensor_tensor_scan(out=end_extra[:, :], data0=big[:, 0:EXPERTS], data1=n_extra[:, :], initial=0.0,
                                      op0=ADD, op1=ADD))
            link(V.tensor_tensor(start_extra[:, :], end_extra[:, :], n_extra[:, :], SUB))
            link(V.tensor_tensor(big[:, :].rearrange("p (b e) -> p b e", e=EXPERTS),
                                 end_extra[:, :].rearrange("p (a e) -> p a e", a=1).broadcast_to([P, 16, EXPERTS]),
                                 iota[:, 0:16].rearrange("p (b a) -> p b a", a=1).broadcast_to([P, 16, EXPERTS]), ALU.is_le))
            link(V.reduce_sum(ctl_f[:, 2:18], big[:, :].rearrange("p (b e) -> p b e", e=EXPERTS), axis=AX.X))
            link(V.tensor_scalar(ctl_f[:, 2:18], ctl_f[:, 2:18], float(EXPERTS - 1), None, ALU.min))
            link(V.memset(ctl_f[:, 1:2], float(EXPERTS - 1)))
            link(V.tensor_copy(ctl_f[:, 0:1], end_extra[:, EXPERTS - 1:EXPERTS]))
            link(V.tensor_copy(control[:, :], ctl_f[:, :]))
            chosen_v = chosen[:, :, :, :].rearrange("p t j e -> p t j e")
            for j in range(2):
                link(V.tensor_tensor(big[:, 256 * j:256 * j + 256].rearrange("p (t e) -> p t e", e=EXPERTS),
                                     bank[7][:, 0:EXPERTS * TILES].rearrange("p (t e) -> p t e", e=EXPERTS),
                                     chosen_v[:, :, j, :], MUL))
                link(V.reduce_sum(rank[:, :].rearrange("p (t j) -> p t j", j=2)[:, :, j],
                                  big[:, 256 * j:256 * j + 256].rearrange("p (t e) -> p t e", e=EXPERTS), axis=AX.X))
            for j in range(2):
                link(V.tensor_tensor(big[:, 256 * j:256 * j + 256].rearrange("p (t e) -> p t e", e=EXPERTS),
                                     start_extra[:, :].rearrange("p (a e) -> p a e", a=1).broadcast_to(
                                         [P, TILES, EXPERTS]), chosen_v[:, :, j, :], MUL))
                link(V.reduce_sum(extra[:, :].rearrange("p (t j) -> p t j", j=2)[:, :, j],
                                  big[:, 256 * j:256 * j + 256].rearrange("p (t e) -> p t e", e=EXPERTS), axis=AX.X))
            link(V.tensor_scalar(level[:, :], rank[:, :], float(P), None, ALU.is_ge))
            for m in range(2, TILES):
                link(V.scalar_tensor_tensor(out=level[:, :], in0=rank[:, :], scalar=float(P * m), in1=level[:, :],
                                            op0=ALU.is_ge, op1=ADD))
            link(V.scalar_tensor_tensor(out=blk[:, :], in0=level[:, :], scalar=float(EXPERTS - 1), in1=extra[:, :],
                                        op0=ADD, op1=ADD))
            experts = expert_of[:, :, :].rearrange("p t j -> p (t j)")
            link(V.tensor_tensor(tmp16[:, :], experts, blk[:, :], SUB))
            link(V.scalar_tensor_tensor(out=tmp16[:, :], in0=level[:, :], scalar=0.0, in1=tmp16[:, :], op0=ALU.is_equal,
                                        op1=MUL))
            link(V.tensor_tensor(blk[:, :], blk[:, :], tmp16[:, :], ADD))
            link(V.scalar_tensor_tensor(out=rank[:, :], in0=level[:, :], scalar=-float(P), in1=rank[:, :], op0=MUL, op1=ADD))
            link(V.scalar_tensor_tensor(out=rank[:, :], in0=rank[:, :], scalar=float(MAX_BLOCKS), in1=blk[:, :], op0=MUL,
                                        op1=ADD))
            V.tensor_copy(address[:, :], rank[:, :]).then_inc(addressed, 1)

            V.memset(xb[:, :], 0.0).then_inc(xb_clear, 1)

            def low_piece(count, slot, raw_slot):
                dve.wait_ge(ew_h_ready, count + 1)
                low(ew_l[slot % SPLIT][:, :], raw[raw_slot][:, :], ew_h[slot % SPLIT][:, :]).then_inc(ew_l_ready, 1)

            def x_low(i):
                dve.wait_ge(xh_ready, i + 1)
                for b in range(2):
                    last = low(xb_l[:, 4 * b:4 * b + 4, :], bank[2 + b][:, :].rearrange("p (k n) -> p k n", n=P),
                               xb_h[:, 4 * b:4 * b + 4, :])
                last.then_inc(xl_ready, 1)

            def activate(i, used):
                dve.wait_ge(silu_done, i + 1)
                dve.wait_ge(ew_used, used)
                V.tensor_tensor(act_row[:, :], silu[:, :], bank[1][:, :], MUL).then_inc(act_done, 1)

            def a_low(i):
                dve.wait_ge(ah_ready, i + 1)
                low(a_l[:, :, :], bank[4][:, :].rearrange("p (k n) -> p k n", n=P), a_h[:, :, :]).then_inc(al_ready, 1)

            for m in range(4):
                low_piece(m, m, (4 + m) % RAW)
            dve.wait_ge(addressed, 1)
            blocks = dve.value_load(control[0:1, 0:1], min_val=0, max_val=MAX_BLOCKS - 1 - EXPERTS) + EXPERTS
            x_low(0)
            for j in range(2):
                low_piece(4 + j, 4 + j, (8 + j) % RAW)
            for j in range(2, 4):
                low_piece(4 + j, 4 + j, (8 + j) % RAW)
                if j == 2:
                    activate(0, 4)
            x_low(1)
            for j in range(4, 6):
                low_piece(4 + j, 4 + j, (8 + j) % RAW)
            a_low(0)

            def step(i, last=False):
                if not last:
                    for j in range(3):
                        low_piece(6 * i + 4 + j, 4 + j, (8 + j) % RAW)
                activate(i, 6 * i + 2)
                if not last:
                    low_piece(6 * i + 7, 7, 11 % RAW)
                x_low(i + 1)
                for j in range(4, 6):
                    if last:
                        low_piece(6 * i + j, j, (4 + j) % RAW)
                    else:
                        low_piece(6 * i + 4 + j, 4 + j, (8 + j) % RAW)
                a_low(i)

            step(1)
            with dve.Fori(2, blocks - 1) as i:
                step(i)
            step(blocks - 1, last=True)


_INS = ["x", "attn_norm_g", "w_in", "sb_q_norm_g", "sb_k_norm_g", "sb_out_norm_g", "gla_gate_w2", "gla_gate_b",
        "gla_out_norm_g", "w_out", "ffn_norm_g", "router_group_w", "router_group_b", "router_expert_w",
        "router_expert_b", "expert_w_gate", "expert_w_up", "expert_w_down"]


def kernel(**inputs):
    import numpy as _np
    import concourse.bacc as _bacc
    from concourse import mybir as _mybir
    from concourse.bass_utils import run_bass_kernel_spmd as _run

    nc = _bacc.Bacc("TRN2", target_bir_lowering=False, num_devices=1)
    arrays, args = {}, []
    for name in _INS:
        a = _np.ascontiguousarray(inputs[name])
        arrays[f"in_{name}"] = a
        args.append(nc.dram_tensor(f"in_{name}", a.shape, _mybir.dt.from_np(a.dtype), kind="ExternalInput").ap())
    out = nc.dram_tensor("out_dram", (1, T, D), _mybir.dt.float32, kind="ExternalOutput").ap()
    hybrid_block_kernel(nc, *args, out)
    r = _run(nc, [arrays], core_ids=[0])
    return r.results[0]["out_dram"]
```

```python
import numpy as np
import concourse.bass as bass
from concourse import mybir
from contextlib import ExitStack

P = 128
D = 1024
T = 1024
TILES = T // P
KT = D // P
HALF = 512
SB_HEADS, SB_DIM = 8, 64
GLA_HEADS, GLA_K, GLA_V = 4, 64, 128
CHUNK = 64
RANK = 16
TAU = 16.0
N_GROUPS, PER_GROUP = 4, 8
EXPERTS = N_GROUPS * PER_GROUP
FF = 512
FT = FF // P
LOGITS = N_GROUPS + EXPERTS
EPS = 1e-6
STEPS = T // P - 1
MOVED = (64, 96, P)
MAX_BLOCKS = 48
NEG = -1e30
GUARD = 80.0
CAP = 16.0
PIECE = 2048
RAW = 6
EARLY = 4
SPLIT = 6
COLS = {"q": 0, "k": 512, "v": 1024, "gqk": 1536, "gv": 2048, "gr": 2560, "glr": 3072}
ORDER = ["gv", "gr", "gqk", "q", "k", "v"]


def hybrid_block_kernel(nc, x, attn_norm_g, w_in, sb_q_norm_g, sb_k_norm_g, sb_out_norm_g, gla_gate_w2,
                        gla_gate_b, gla_out_norm_g, w_out, ffn_norm_g, router_group_w, router_group_b,
                        router_expert_w, router_expert_b, expert_w_gate, expert_w_up, expert_w_down, out):
    fp32, f32r, bf16, u32, i32 = (mybir.dt.float32, mybir.dt.float32r, mybir.dt.bfloat16, mybir.dt.uint32,
                                  mybir.dt.int32)
    ALU, ACT, AX = mybir.AluOpType, mybir.ActivationFunctionType, mybir.AxisListType
    ADD, SUB, MUL = ALU.add, ALU.subtract, ALU.mult

    gv_dram = nc.dram_tensor("gv_dram", (TILES, P, HALF), fp32, kind="Internal").ap()
    gr_dram = nc.dram_tensor("gr_dram", (TILES, P, HALF), fp32, kind="Internal").ap()
    v_dram = nc.dram_tensor("v_dram", (T, D), fp32, kind="Internal").ap()

    x_t = x[0].rearrange("(t p) d -> t p d", p=P)
    out_rows = out[0]
    out_t = out_rows.rearrange("(t p) d -> t p d", p=P)
    w_in_v = w_in[0].rearrange("(p k) n -> p k n", k=KT)
    w_out_v = w_out[0].rearrange("(k p) n -> p k n", p=P)
    gate_v = expert_w_gate[0].rearrange("e (p k) n -> e p (k n)", k=KT)
    up_v = expert_w_up[0].rearrange("e (p k) n -> e p (k n)", k=KT)
    down_v = expert_w_down[0].rearrange("e (p k) n -> e p (k n)", k=FT)

    ctx = ExitStack()
    with ctx:
        def const(name, shape, dt=fp32):
            return ctx.enter_context(nc.sbuf_tensor(name, shape, dt))

        def sem(name):
            return ctx.enter_context(nc.semaphore(name))

        ident = const("ident", [P, P])
        ident_b = const("ident_b", [P, P], bf16)
        causal_neg = const("causal_neg", [P, P], bf16)
        tri_f = const("tri_f", [P, P])
        tri_neg = const("tri_neg", [P, P], f32r)
        ones_neg = const("ones_neg", [P, P])
        head_mean = const("head_mean", [P, P])
        suffix = const("suffix", [P, P])
        chunk_sel = const("chunk_sel", [P, 2])
        before = const("before", [P, P], bf16)
        ones_b = const("ones_b", [P, P], bf16)
        iota = const("iota", [P, P])
        steps = const("steps", [P, STEPS])
        zeros = const("zeros", [P, EXPERTS])
        eps_col = const("eps_col", [P, 1])
        gate_w2 = const("gate_w2", [RANK + 1, 256])
        gla_gain = const("gla_gain", [P, GLA_V])
        router_bias = const("router_bias", [P, LOGITS])
        q_gain = const("q_gain", [P, 1])
        k_gain = const("k_gain", [P, 1])
        o_gain = const("o_gain", [P, SB_HEADS // 2])
        router_w = const("router_w", [P, KT, LOGITS])
        stat = const("stat", [P, 16])
        row_sum = const("row_sum", [P, TILES])
        row_mean = const("row_mean", [P, TILES])
        row_rstd = const("row_rstd", [P, TILES])
        grp_logits = const("grp_logits", [P, 8])
        top_val = const("top_val", [P, 2, 8])
        top_idx = const("top_idx", [P, 2, 8], u32)
        chosen = const("chosen", [P, TILES, 2, EXPERTS], bf16)
        chosen_any = const("chosen_any", [P, TILES, EXPERTS], bf16)
        expert_of = const("expert_of", [P, TILES, 2])
        payload = const("payload", [P, TILES, 2, 2])
        control = const("control", [P, 2 + 16 + MAX_BLOCKS], i32)
        table = const("table", [P, MAX_BLOCKS, 2], u32)
        exp_logits = const("exp_logits", [P, EXPERTS])
        masked = const("masked", [P, EXPERTS])
        sel_logits = const("sel_logits", [P, 8])
        r_small = const("r_small", [P, 18])
        gather_idx = const("gather_idx", [P, 1], u32)
        scatter_row = const("scatter_row", [P, 2], u32)

        base = (nc.sbuf_usable_end - nc.sbuf_bytes_remaining + 63) // 64 * 64
        KB = 1024
        R1, R2, R3 = base, base + 64 * KB, base + 128 * KB
        RAWS = R3 + 20 * KB
        assert RAWS + 48 * KB <= nc.sbuf_usable_end, (base, nc.sbuf_usable_end)

        def at(name, offset, shape, dt=fp32):
            return nc.alloc_sbuf_tensor_at(name, shape, dt, offset=offset)

        q_t = at("q_t", R1, [P, 4, T])
        k_t = at("k_t", R1 + 16 * KB, [P, 4, T])
        v_s = at("v_s", R1 + 32 * KB, [P, TILES, HALF])
        gq_t = at("gq_t", R1 + 48 * KB, [P, 2, T])
        gk_t = at("gk_t", R1 + 56 * KB, [P, 2, T])
        u_h = at("u_h", R2, [P, KT, T], f32r)
        u_l = at("u_l", R2 + 32 * KB, [P, KT, T], f32r)
        win_raw = [at(f"win_raw{i}", R3 + 8 * KB * i, [P, PIECE]) for i in range(2)]
        win_h = [at(f"win_h{i}", R3 + (16 + 8 * i) * KB, [P, 4, HALF], f32r) for i in range(2)]
        win_l = [at(f"win_l{i}", R3 + (32 + 8 * i) * KB, [P, 4, HALF], f32r) for i in range(2)]
        x_in = [at(f"x_in{i}", R1 + 4 * KB * i, [P, D]) for i in range(TILES)]
        u_row = [at(f"u_row{i}", R1 + (32 + 4 * i) * KB, [P, D]) for i in range(2)]
        squares = at("squares", R1 + 40 * KB, [P, D])
        gain1 = at("gain1", R1 + 44 * KB, [P, D])
        spill = [at(f"spill{i}", R3 + (64 + 2 * i) * KB, [P, HALF]) for i in range(2)]
        glr_raw = at("glr_raw", R3 + 48 * KB, [P, KT, P])
        glr_h = at("glr_h", R3 + 52 * KB, [P, KT, P], f32r)
        glr_l = at("glr_l", R3 + 60 * KB, [P, KT, P], f32r)
        mix_h = at("mix_h", R2, [P, KT, T], f32r)
        mix_l = at("mix_l", R2 + 32 * KB, [P, KT, T], f32r)
        place = [R3]

        def nxt(name, n, dt=fp32, shape=None):
            t = at(name, place[0], shape or [P, n], dt)
            place[0] += n * 4
            return t

        o_s = nxt("o_s", HALF)
        sq = [nxt(f"sq{i}", HALF) for i in range(2)]
        rs = [nxt(f"rs{i}", HALF) for i in range(2)]
        gv_s = nxt("gv_s", HALF)
        gr_s = nxt("gr_s", HALF)
        gsig = nxt("gsig", HALF)
        go = nxt("go", HALF)
        gstat = nxt("gstat", 32)
        assert place[0] <= RAWS
        gk_s = nxt("gk_s", 256)
        k_dec = nxt("k_dec", 256)
        log_g = nxt("log_g", 256)
        prob = [nxt(f"prob{i}", HALF) for i in range(2)]
        soft = [nxt(f"soft{i}", HALF) for i in range(2)]
        sp = [nxt(f"sp{i}", HALF) for i in range(3)]
        sp_h = [nxt(f"sp_h{i}", HALF, f32r) for i in range(3)]
        sp_l = [nxt(f"sp_l{i}", HALF, f32r) for i in range(3)]
        later = [nxt(f"later{i}", HALF) for i in range(3)]
        state = [nxt(f"state{i}", HALF, shape=[P, 2, 256]) for i in range(3)]
        assert place[0] <= R3 + 60 * KB, place[0] - R3
        glr_t = at("glr_t", R2 + (32 + 4 * 3) * KB, [RANK + 1, T])
        wo_h = at("wo_h", R1, [P, KT, D], f32r)
        wo_l = at("wo_l", R1 + 32 * KB, [P, KT, D], f32r)
        h_row = [at(f"h_row{i}", R3 + 4 * KB * i, [P, D]) for i in range(2)]
        v_row = at("v_row", R3 + 8 * KB, [P, D])
        v_t = at("v_t", R3 + 12 * KB, [P, KT, P])
        gain2 = at("gain2", R3 + 16 * KB, [P, D])
        raw = [at(f"raw{i}", RAWS + (40 * KB if i == 0 else 8 * KB * (i - 1)), [P, PIECE]) for i in range(RAW)]
        raw += [at(f"raw{RAW + i}", R3 + 8 * KB * i, [P, PIECE]) for i in range(2)]
        ew_h = [at(f"ew_h{i}", R1 + 16 * KB * i, [P, PIECE], f32r) for i in range(SPLIT)]
        ew_l = [at(f"ew_l{i}", R1 + 16 * KB * i + 8 * KB, [P, PIECE], f32r) for i in range(SPLIT)]
        M = R1 + 96 * KB
        xb = at("xb", M, [P, D])
        xb_h = at("xb_h", M + 4 * KB, [P, KT, P], f32r)
        xb_l = at("xb_l", M + 8 * KB, [P, KT, P], f32r)
        silu = at("silu", M + 12 * KB, [P, FF])
        act_row = at("act_row", M + 14 * KB, [P, FF])
        a_h = at("a_h", M + 16 * KB, [P, FT, P], f32r)
        a_l = at("a_l", M + 18 * KB, [P, FT, P], f32r)
        y_row = at("y_row", M + 20 * KB, [P, D])
        row_hot = at("row_hot", M + 4 * KB, [P, 2 * TILES, P])
        block_hot = at("block_hot", M + 12 * KB, [P, 2 * TILES, MAX_BLOCKS])
        entries = at("entries", M + 16 * KB, [P, 2 * TILES, 2, MAX_BLOCKS])
        place[0] = M + 24 * KB
        by_expert = nxt("by_expert", 2 * TILES * EXPERTS)
        over = nxt("over", EXPERTS * STEPS)
        over_row = nxt("over_row", 2 * TILES * STEPS)
        rank, block_row, extra, level, blk, moved = (nxt(name, 16) for name in ("rank", "block_row", "extra", "level", "blk", "moved"))
        n_extra = nxt("n_extra", EXPERTS)
        end_extra = nxt("end_extra", EXPERTS)
        start_extra = nxt("start_extra", EXPERTS)
        ctl_f = nxt("ctl_f", 18 + MAX_BLOCKS)
        assert place[0] <= R1 + 128 * KB

        bank = [ctx.enter_context(nc.psum_tensor(f"bank{i}", [P, HALF], fp32)) for i in range(8)]

        fixed = sem("fixed")
        consts_in = sem("consts_in")
        gain_in = sem("gain_in")
        xs = [sem(f"x_loaded{i}") for i in range(TILES)]
        small = sem("small")
        asmall = sem("asmall")
        psmall = sem("psmall")
        square_done, mean_done, rstd_done = sem("square_done"), sem("mean_done"), sem("rstd_done")
        u_ready, x_gained, u_turned, uh_ready, ul_ready = sem("u_ready"), sem("x_gained"), sem("u_turned"), sem("uh_ready"), sem("ul_ready")
        win_in = [sem(f"win_loaded{i}") for i in range(2)]
        win_h_ready, win_l_ready, win_used = sem("win_h_ready"), sem("win_l_ready"), sem("win_used")
        unit_done, unit_out = sem("unit_done"), sem("unit_out")
        spilled = [sem(f"spilled{i}") for i in range(2)]
        glr_in, glr_split, glr_done, glr_out = sem("glr_in"), sem("glr_split"), sem("glr_done"), sem("glr_out")
        glr_ones = sem("glr_ones")
        qk_done, ln_done = sem("qk_done"), sem("ln_done")
        sp_done, spl_done, later_done = sem("sp_done"), sem("spl_done"), sem("later_done")
        tail_done, prob_done, pv_done = sem("tail_done"), sem("prob_done"), sem("pv_done")
        sq_done, ms_done, rln_done, rs_done = sem("sq_done"), sem("ms_done"), sem("rln_done"), sem("rs_done")
        o_out, q_normed, mix_ready = sem("o_out"), sem("q_normed"), sem("mix_ready")
        gvr_in, g_turned, g_turned_out, g_logit = sem("gvr_in"), sem("g_turned"), sem("g_turned_out"), sem("g_logit")
        g_cap, g_ln, g_log, g_decay, g_exp = sem("g_cap"), sem("g_ln"), sem("g_log"), sem("g_decay"), sem("g_exp")
        g_kdec, g_kv, g_state, g_o = sem("g_kdec"), sem("g_kv"), sem("g_state"), sem("g_o")
        g_rcap, g_sig_part, g_sig, g_silu, g_gain, g_sq, g_ms, g_rs = (sem("g_rcap"), sem("g_sig_part"), sem("g_sig"), sem("g_silu"), sem("g_gain"), sem("g_sq"),
                                                   sem("g_ms"), sem("g_rs"))
        g_go, g_got, g_mixh, g_mixl = sem("g_go"), sem("g_got"), sem("g_mixh"), sem("g_mixl")
        raw_in = [sem(f"raw_loaded{i}") for i in range(RAW + 2)]
        wo_h_ready, wo_l_ready = sem("wo_h_ready"), sem("wo_l_ready")
        hx = [sem(f"h_x_loaded{i}") for i in range(2)]
        gain2_in = sem("gain2_in")
        wo_done, h_ready, h_square, h_mean, h_rstd, v_ready = (sem("wo_done"), sem("h_ready"), sem("h_square"),
                                                               sem("h_mean"), sem("h_rstd"), sem("v_ready"))
        h_stored = [sem(f"h_stored{i}") for i in range(2)]
        v_stored = sem("v_stored")
        v_turned, vt_ready, logit_done, logit_out = (sem("v_turned"), sem("vt_ready"), sem("logit_done"),
                                                     sem("logit_out"))
        r_max, r_exp, r_diff, r_ratio, routed = sem("r_max"), sem("r_exp"), sem("r_diff"), sem("r_ratio"), sem("routed")
        ranked, row_hot_ready = sem("ranked"), sem("row_hot_ready")
        entries_ready, table_done, table_ready = sem("entries_ready"), sem("table_done"), sem("table_ready")
        control_ready = sem("control_ready")
        ew_h_ready, ew_l_ready, ew_used = sem("ew_h_ready"), sem("ew_l_ready"), sem("ew_used")
        rows_in, idx_ready, x_turned, xh_ready, xl_ready = (sem("rows_in"), sem("idx_ready"), sem("x_turned"),
                                                            sem("xh_ready"), sem("xl_ready"))
        xb_clear = sem("xb_clear")
        silu_done, act_done = sem("silu_done"), sem("act_done")
        a_turned, ah_ready, al_ready = sem("a_turned"), sem("ah_ready"), sem("al_ready")
        row_ready, y_ready, y_added = sem("row_ready"), sem("y_ready"), sem("y_added")

        N_CONSTS = 12
        units = []
        for pair in range(4):
            for qc in (1, 0):
                for hd in (2 * pair, 2 * pair + 1):
                    js = list(range(4 * qc + 3, -1, -1))
                    for j in js:
                        q0 = HALF * qc
                        units.append(dict(pair=pair, qc=qc, hd=hd, j=j, first=j == js[0], last=j == 0,
                                          lo=max(P * j, q0) - q0, diag=P * j >= q0))
        NU = len(units)
        PER_PAIR = NU // 4
        GROUP_END = {PER_PAIR * p + e: 2 * p + g for p in range(4) for g, e in enumerate((15, 23))}
        WINDOW = NU // TILES
        SLOT_END = NU + 9
        DRAIN, WO_EARLY = NU + 4, 2
        QN = 4
        QK_SLOTS = (6, 9, 12, 15)

        W_ORDER = [(n + 4) % TILES for n in range(TILES)]

        def raw_slot(m):
            if m in (12, 13):
                return RAW + m - 12
            return (m + 4) % RAW if m < 12 else (m + 2) % RAW

        def raw_count(m):
            return sum(raw_slot(k) == raw_slot(m) for k in range(m + 1)) + (raw_slot(m) < 4)

        def laters(n):
            return sum(not u["last"] for u in units[:n])

        def unit_bank(u):
            return bank[(u + 4) % 8]

        block = ctx.enter_context(nc.Block())

        def norm_event(s):
            p, r = divmod(s, PER_PAIR)
            if p < 3 and r in QK_SLOTS:
                return p + 1, QK_SLOTS.index(r)
            return None

        norm_order = {("qk", 0, b): b for b in range(QN)}
        for s in range(SLOT_END):
            if s >= 5 and s - 5 in GROUP_END:
                norm_order[("o", GROUP_END[s - 5])] = len(norm_order)
            if s >= 1 and norm_event(s - 1):
                norm_order[("qk", *norm_event(s - 1))] = len(norm_order)

        def qk_block(b, pair):
            src = (q_t, k_t)[b // 2]
            return src[:, pair, HALF * (b % 2):HALF * (b % 2) + HALF]

        @block.sync
        def _(sp_e):
            def load_win(n):
                c0 = COLS[ORDER[n // 2]]
                sp_e.dma_start(win_raw[n % 2][:, :].rearrange("p (k n) -> p k n", n=HALF),
                               w_in_v[:, 4 * (n % 2):4 * (n % 2) + 4, c0:c0 + HALF]).then_inc(win_in[n % 2], 16)

            for t in range(TILES):
                sp_e.dma_start(x_in[t][:, :], x_t[t]).then_inc(xs[t], 16)
                if t == 1:
                    sp_e.dma_start(gain1[:, :], attn_norm_g[0:1, :].partition_broadcast(P)).then_inc(gain_in, 16)
            load_win(0)
            load_win(1)
            sp_e.wait_ge(fixed, 1)
            sp_e.dma_start(glr_raw[:, :, 0:RANK], w_in_v[:, :, COLS["glr"]:COLS["glr"] + RANK]).then_inc(glr_in, 16)
            c = [0]

            def load(dst, src):
                c[0] += 1
                sp_e.dma_start(dst, src, allow_slow_non_contiguous=True).then_inc(consts_in, 16)

            load(gate_w2[0:RANK, :], gla_gate_w2[0])
            load(gate_w2[RANK:RANK + 1, :], gla_gate_b)
            load(gla_gain[:, :], gla_out_norm_g.partition_broadcast(P))
            load(router_bias[:, 0:N_GROUPS], router_group_b.partition_broadcast(P))
            load(router_bias[:, N_GROUPS:LOGITS], router_expert_b.partition_broadcast(P))
            for r in range(2):
                load(q_gain[SB_DIM * r:SB_DIM * (r + 1), :], sb_q_norm_g.rearrange("a d -> d a"))
                load(k_gain[SB_DIM * r:SB_DIM * (r + 1), :], sb_k_norm_g.rearrange("a d -> d a"))
                load(o_gain[SB_DIM * r:SB_DIM * (r + 1), :],
                     sb_out_norm_g[0].rearrange("(a b) d -> b d a", b=2)[r])
            load(router_w[:, :, 0:N_GROUPS], router_group_w[0].rearrange("(p k) n -> p k n", k=KT))
            sp_e.dma_start(router_w[:, :, N_GROUPS:LOGITS],
                           router_expert_w[0].rearrange("(p k) n -> p k n", k=KT)).then_inc(consts_in, 16)
            assert c[0] == N_CONSTS
            for n in range(2, 2 * len(ORDER)):
                sp_e.wait_ge(win_l_ready, n - 1)
                load_win(n)
            sp_e.wait_ge(glr_done, 2)
            sp_e.wait_ge(glr_out, 2)
            for i in range(2):
                sp_e.wait_ge(spilled[i], 16 * TILES)
            sp_e.dma_start(raw[0][:, :].rearrange("p (k n) -> p k n", n=D), w_out_v[:, 0:2, :]).then_inc(raw_in[0], 16)
            for t in range(TILES):
                if t:
                    sp_e.wait_ge(g_kv, 2 * t)
                    sp_e.wait_ge(g_silu, t)
                sp_e.dma_start(gv_s[:, :], gv_dram[t]).then_inc(gvr_in, 16)
                sp_e.dma_start(gr_s[:, :], gr_dram[t]).then_inc(gvr_in, 16)
            sp_e.wait_ge(pv_done, NU)
            for n in range(1, 4):
                sp_e.dma_start(raw[n][:, :].rearrange("p (k n) -> p k n", n=D),
                               w_out_v[:, 2 * n:2 * n + 2, :]).then_inc(raw_in[n], 16)
            sp_e.wait_ge(mix_ready, 8)
            sp_e.wait_ge(g_mixh, TILES)
            sp_e.wait_ge(g_mixl, TILES)
            for n in range(2):
                sp_e.dma_start(h_row[n][:, :], x_t[W_ORDER[n]]).then_inc(hx[n], 16)
            sp_e.dma_start(gain2[:, :], ffn_norm_g.partition_broadcast(P)).then_inc(gain2_in, 16)

            def load_piece(slot, src):
                sp_e.dma_start(raw[slot][:, :], src).then_inc(raw_in[slot], 16)

            def gate_up(e, j):
                v = (gate_v, up_v)[j // 2]
                return v[e][:, PIECE * (j % 2):PIECE * (j % 2 + 1)]

            for j in range(4):
                if j >= 2:
                    sp_e.wait_ge(wo_l_ready, j - 1)
                load_piece(raw_slot(j), gate_up(0, j))
            for j in range(2):
                sp_e.wait_ge(wo_l_ready, j + 3)
                load_piece(raw_slot(4 + j), gate_up(1, j))
            for t in range(TILES):
                sp_e.wait_ge(v_ready, t + 1)
                a = W_ORDER[t]
                sp_e.dma_start(out_t[a], h_row[t % 2][:, :]).then_inc(h_stored[t % 2], 16)
                sp_e.dma_start(v_dram[P * a:P * (a + 1), :], v_row[:, :]).then_inc(v_stored, 16)
                if t + 2 < TILES:
                    sp_e.wait_ge(h_stored[t % 2], 16 * (t // 2 + 1))
                    sp_e.dma_start(h_row[t % 2][:, :], x_t[W_ORDER[t + 2]]).then_inc(hx[t % 2], 16)
            for j in range(2, 6):
                sp_e.wait_ge(ew_l_ready, j - 1)
                load_piece(raw_slot(4 + j), gate_up(1, j) if j < 4 else down_v[0][:, PIECE * (j - 4):PIECE * (j - 3)])
            for m in range(10, 22):
                i, j = (m + 2) // 6, (m + 2) % 6
                if m == 12:
                    sp_e.wait_ge(logit_done, TILES)
                    sp_e.wait_ge(v_turned, TILES)
                    sp_e.wait_ge(v_stored, 16 * TILES)
                    for k in range(2):
                        sp_e.wait_ge(h_stored[k], 16 * TILES // 2)
                elif m != 13:
                    sp_e.wait_ge(ew_l_ready, m - 7 if 14 <= m < 20 else m - 5)
                load_piece(raw_slot(m), gate_up(i, j) if j < 4 else down_v[i - 1][:, PIECE * (j - 4):PIECE * (j - 3)])

            def expert_pieces(i, e, before_e):
                for j in range(6):
                    sp_e.wait_ge(ew_l_ready, 6 * i + j - 7)
                    if j < 4:
                        v = (gate_v, up_v)[j // 2]
                        src = v[bass.ds(e, 1), :, PIECE * (j % 2):PIECE * (j % 2 + 1)]
                    else:
                        src = down_v[bass.ds(before_e, 1), :, PIECE * (j - 4):PIECE * (j - 3)]
                    sp_e.dma_start(raw[j][:, :], src.rearrange("e p n -> p (e n)")).then_inc(raw_in[j], 16)

            with sp_e.Fori(4, EXPERTS) as i:
                expert_pieces(i, i, i - 1)
            sp_e.wait_ge(control_ready, 1)
            blocks = sp_e.value_load(control[0:1, 0:1], min_val=0, max_val=MAX_BLOCKS - 1 - EXPERTS) + EXPERTS
            with sp_e.If(blocks > EXPERTS):
                with sp_e.Fori(EXPERTS, blocks) as i:
                    e_now = sp_e.value_load(control[0:1, bass.ds(i - EXPERTS + 2, 1)], min_val=0, max_val=EXPERTS - 1)
                    e_old = sp_e.value_load(control[0:1, bass.ds(i - EXPERTS + 1, 1)], min_val=0, max_val=EXPERTS - 1)
                    expert_pieces(i, e_now, e_old)
            e_last = sp_e.value_load(control[0:1, bass.ds(blocks - EXPERTS + 1, 1)], min_val=0, max_val=EXPERTS - 1)
            for j in range(2):
                sp_e.wait_ge(ew_l_ready, 6 * blocks + j - 7)
                sp_e.dma_start(raw[j][:, :],
                               down_v[bass.ds(e_last, 1), :, PIECE * j:PIECE * (j + 1)].rearrange(
                                   "e p n -> p (e n)")).then_inc(raw_in[j], 16)
            sp_e.wait_ge(v_stored, 16 * TILES)

        @block.gpsimd
        def _(pool):
            chain = [0]

            def link(ins):
                chain[0] += 1
                ins.then_inc(psmall, 1)
                pool.wait_ge(psmall, chain[0])

            for tile, value in ((ident, 0.0), (causal_neg, 0.0), (tri_f, -1.0), (ones_neg, -1.0), (head_mean, 0.0),
                                (suffix, 0.0), (chunk_sel, 0.0), (before, 1.0), (ones_b, 1.0), (eps_col, EPS)):
                last = nc.gpsimd.memset(tile[:, :], value)
            nc.gpsimd.memset(glr_raw[:, :, :], 0.0)
            last = nc.gpsimd.memset(grp_logits[:, :], NEG)
            link(last)
            for b in range(2):
                r = slice(64 * b, 64 * b + 64)
                nc.gpsimd.memset(head_mean[r, r], 1.0 / SB_DIM)
                nc.gpsimd.memset(suffix[r, r], 1.0 / TAU)
                last = nc.gpsimd.memset(chunk_sel[r, b:b + 1], 1.0 / TAU)
            link(last)

            def triangle(tile, fill, op, sign):
                return nc.gpsimd.affine_select(out=tile[:, :], in_=tile[:, :], compare_op=op, fill=fill, base=0,
                                               pattern=[[-sign, P]], channel_multiplier=sign)

            triangle(ident, 1.0, ALU.not_equal, 1)
            triangle(causal_neg, NEG, ALU.is_gt, -1)
            triangle(tri_f, 0.0, ALU.is_ge, 1)
            triangle(suffix, 0.0, ALU.is_gt, 1)
            link(triangle(before, 0.0, ALU.is_gt, -1))
            nc.gpsimd.memset(zeros[:, :], 0.0)
            nc.gpsimd.iota(steps[:, :], pattern=[[P, STEPS]], base=P, channel_multiplier=0,
                           allow_small_or_imprecise_dtypes=True)
            nc.gpsimd.iota(iota[:, :], pattern=[[1, P]], base=0, channel_multiplier=0,
                           allow_small_or_imprecise_dtypes=True)
            nc.gpsimd.iota(payload[:, :, :, 0], pattern=[[-P, TILES], [0, 2]], base=T, channel_multiplier=-1,
                           allow_small_or_imprecise_dtypes=True).then_inc(fixed, 1)

            pool.wait_ge(gain_in, 16)
            for t in range(1, TILES):
                pool.wait_ge(square_done, t + 1)
                nc.gpsimd.tensor_tensor(x_in[t][:, :], x_in[t][:, :], gain1[:, :], MUL).then_inc(x_gained, 1)

            for s in range(1, NU + 1):
                n, u = s - 1, units[s - 1]
                if not u["last"]:
                    pool.wait_ge(sp_done, n + 1)
                    if s == 1:
                        for i in range(3):
                            nc.gpsimd.memset(state[i][:, :, :], 0.0)
                    if n >= 3:
                        pool.wait_ge(tail_done, n - 1)
                    new, old, lo = later[n % 3], later[(n - 1) % 3], u["lo"]
                    mid = lo + P if u["diag"] else lo
                    if laters(n):
                        pool.wait_ge(later_done, laters(n))
                    if u["diag"]:
                        last = nc.gpsimd.tensor_copy(new[:, lo:mid], sp[n % 3][:, lo:mid])
                    if not u["first"]:
                        last = nc.gpsimd.tensor_tensor(new[:, mid:HALF], old[:, mid:HALF], sp[n % 3][:, mid:HALF], ADD)
                    last.then_inc(later_done, 1)
                if s % WINDOW == 10:
                    t = s // WINDOW
                    pool.wait_ge(g_silu, t + 1)
                    nc.gpsimd.tensor_tensor(gsig[:, :].rearrange("p (h n) -> p h n", n=GLA_V),
                                            gsig[:, :].rearrange("p (h n) -> p h n", n=GLA_V),
                                            gla_gain[:, :].rearrange("p (a n) -> p a n", a=1).broadcast_to(
                                                [P, GLA_HEADS, GLA_V]), MUL).then_inc(g_gain, 1)

            for m in range(4):
                pool.wait_ge(ew_h_ready, m + 1)
                nc.gpsimd.tensor_tensor(ew_l[m][:, :], raw[raw_slot(m)][:, :], ew_h[m][:, :].bitcast(fp32),
                                        SUB).then_inc(ew_l_ready, 1)
            pool.wait_ge(v_stored, 16 * TILES)
            for i in range(2):
                pool.wait_ge(h_stored[i], 16 * TILES // 2)
            pool.wait_ge(xb_clear, 1)
            pool.wait_ge(table_ready, 1)
            pool.wait_ge(control_ready, 1)

            def held(semaphore, value):
                value = value if isinstance(value, int) else pool.to_reg(value)
                pool.wait_ge(table_ready, 1)
                pool.wait_ge(semaphore, value)

            def by_size(i, move):
                size = pool.value_load(control[0:1, bass.ds(i + 18, 1)], min_val=0, max_val=2)
                with pool.If(size > 1):
                    move(MOVED[2])
                with pool.Else():
                    with pool.If(size > 0):
                        move(MOVED[1])
                    with pool.Else():
                        move(MOVED[0])

            def gather(i):
                nc.gpsimd.tensor_copy(gather_idx[:, :], table[:, bass.ds(i, 1), 0]).then_inc(idx_ready, 1)
                held(idx_ready, i + 1)

                def move(n):
                    pool.indirect_dma_start(out=xb[0:n, :], out_offset=None, in_=v_dram,
                                            in_offset=bass.IndirectOffsetOnAxis(ap=gather_idx[0:n, :], axis=0),
                                            bounds_check=T - 1, oob_is_err=False).then_inc(rows_in, 16)
                by_size(i, move)

            def rows(i):
                nc.gpsimd.tensor_copy(scatter_row[:, :], table[:, bass.ds(i, 1), :].rearrange("p a c -> p (a c)")).then_inc(row_ready, 1)

            def scatter(i):
                def move(n):
                    pool.indirect_dma_start(out=out_rows, out_offset=bass.IndirectOffsetOnAxis(ap=scatter_row[0:n, 0:1], axis=0),
                                            in_=y_row[0:n, :], in_offset=None, bounds_check=T - 1, oob_is_err=False,
                                            compute_op=ADD).then_inc(y_added, 16)
                by_size(i, move)

            gather(0)
            rows(0)
            for i in range(1, 4):
                pool.wait_ge(x_turned, i)
                gather(i)
            pool.wait_ge(y_ready, 1)
            scatter(0)
            blocks = pool.value_load(control[0:1, 0:1], min_val=0, max_val=MAX_BLOCKS - 1 - EXPERTS) + EXPERTS
            with pool.Fori(2, blocks - 2) as i:
                held(x_turned, i + 2)
                gather(i + 2)
                held(y_added, 16 * (i - 1))
                rows(i - 1)
                held(y_ready, i)
                scatter(i - 1)
            for back in (3, 2, 1):
                held(y_added, 16 * (blocks - back))
                rows(blocks - back)
                held(y_ready, blocks - back + 1)
                scatter(blocks - back)
            held(y_added, 16 * blocks)

        @block.tensor
        def _(pe):
            mm = nc.tensor.matmul

            def three(ps, lh, ll, rh, rl, start, stop):
                mm(ps, lh, rh, start=start, stop=False)
                mm(ps, lh, rl, start=False, stop=False)
                return mm(ps, ll, rh, start=False, stop=stop)

            def project(n, u):
                name, wh, wl = ORDER[n // 2], win_h[n % 2], win_l[n % 2]
                for kk in range(4):
                    k = 4 * (n % 2) + kk
                    flags = dict(start=k == 0, stop=k == KT - 1)
                    if name in ("gv", "gr", "v"):
                        tok = slice(P * u, P * u + P)
                        last = three(unit_bank(u)[:, :], u_h[:, k, tok], u_l[:, k, tok], wh[:, kk, :], wl[:, kk, :], **flags)
                    else:
                        col, tok = slice(P * (u // 2), P * (u // 2) + P), slice(HALF * (u % 2), HALF * (u % 2) + HALF)
                        last = three(unit_bank(u)[:, :], wh[:, kk, col], wl[:, kk, col], u_h[:, k, tok], u_l[:, k, tok], **flags)
                return last

            pe.wait_ge(fixed, 1)
            for t in range(TILES):
                pe.wait_ge(u_ready, t + 1)
                if t >= 2:
                    pe.wait_ge(uh_ready, t - 1)
                    pe.wait_ge(ul_ready, t - 1)
                rows = u_row[t % 2][:, :].rearrange("p (d k) -> p k d", k=KT)
                for k in range(KT):
                    last = nc.tensor.transpose(bank[2 * (t % 2) + k // 4][:, P * (k % 4):P * (k % 4 + 1)], rows[:, k, :],
                                               ident[:, :])
                last.then_inc(u_turned, 1)
                if t >= EARLY:
                    if t == EARLY:
                        pe.wait_ge(win_l_ready, 1)
                    project(0, t - EARLY)

            for n in range(2 * len(ORDER)):
                c = n // 2
                pe.wait_ge(win_l_ready, n + 1)
                if n == 0:
                    pe.wait_ge(ul_ready, TILES)
                for u in range(TILES - EARLY if n == 0 else 0, 8):
                    if n % 2 == 0 and c:
                        pe.wait_ge(unit_out, 8 * (c - 1) + u + 1)
                    last = project(n, u)
                    if n % 2:
                        last.then_inc(unit_done, 1)
                    elif u == 7:
                        last.then_inc(win_used, 1)

            def head_norm(key):
                pe.wait_ge(sq_done, norm_order[key] + 1)
                n = norm_order[key]
                if n:
                    pe.wait_ge(rln_done, n)
                mm(bank[7][:, :], head_mean[:, :], sq[n % 2][:, :], start=True, stop=True).then_inc(ms_done, 1)

            pe.wait_ge(glr_split, 2)
            for b in range(2):
                pe.wait_ge(unit_out, 8 * (len(ORDER) - 1) + b + 1)
                tok = slice(HALF * b, HALF * b + HALF)
                for k in range(KT):
                    last = three(unit_bank(b)[:, :], glr_h[:, k, :], glr_l[:, k, :], u_h[:, k, tok], u_l[:, k, tok],
                                 start=k == 0, stop=k == KT - 1)
                last.then_inc(glr_done, 1)
                head_norm(("qk", 0, b))
            for b in range(2, QN):
                head_norm(("qk", 0, b))

            pe.wait_ge(consts_in, 16 * (N_CONSTS + 1))
            pe.wait_ge(glr_out, 2)
            pe.wait_ge(fixed, 2)
            for s in range(SLOT_END):
                if s < NU:
                    u = units[s]
                    row, q0 = slice(64 * (u["hd"] % 2), 64 * (u["hd"] % 2) + 64), HALF * u["qc"]
                    pe.wait_ge(q_normed, 4 * u["pair"] + 4)
                    if s >= 4:
                        pe.wait_ge(prob_done, s - 3)
                    z = bank[s % 4][:, u["lo"]:HALF]
                    last = mm(z, k_t[row, u["pair"], P * u["j"]:P * u["j"] + P],
                              q_t[row, u["pair"], q0 + u["lo"]:q0 + HALF], start=True, stop=True)
                    if u["diag"]:
                        last = mm(bank[s % 4][:, u["lo"]:u["lo"] + P], ident_b[:, :], causal_neg[:, :], start=False,
                                  stop=True, skip_group_check=True)
                    last.then_inc(qk_done, 1)
                if 2 <= s and s - 2 < NU:
                    n, u = s - 2, units[s - 2]
                    z = bank[n % 4][:, u["lo"]:HALF]
                    mid = u["lo"] + P if u["diag"] else u["lo"]
                    if not u["first"]:
                        pe.wait_ge(sp_done, n + 1)
                        pe.wait_ge(later_done, laters(n))
                        mm(bank[n % 4][:, mid:HALF], ones_neg[:, :], later[(n - 1) % 3][:, mid:HALF], start=False,
                           stop=True, skip_group_check=True)
                    pe.wait_ge(spl_done, n + 1)
                    mm(z, tri_neg[:, :], sp_h[n % 3][:, u["lo"]:HALF], start=False, stop=True, skip_group_check=True)
                    last = mm(z, tri_neg[:, :], sp_l[n % 3][:, u["lo"]:HALF], start=False, stop=True,
                              skip_group_check=True)
                    last.then_inc(tail_done, 1)
                if 3 <= s and s - 3 < NU:
                    n, u = s - 3, units[s - 3]
                    pe.wait_ge(prob_done, n + 1)
                    half = slice(64 * (u["hd"] % 2), 64 * (u["hd"] % 2) + 64)
                    g = 2 * u["pair"] + (u["qc"] == 0)
                    if u["first"] and g:
                        pe.wait_ge(o_out, g)
                    mm(bank[4][half, u["lo"]:HALF], v_s[:, u["j"], SB_DIM * u["hd"]:SB_DIM * (u["hd"] + 1)],
                       prob[n % 2][:, u["lo"]:HALF], start=u["first"], stop=u["last"],
                       skip_group_check=True).then_inc(pv_done, 1)
                if s >= 5 and s - 5 in GROUP_END:
                    head_norm(("o", GROUP_END[s - 5]))
                if s >= 1 and norm_event(s - 1):
                    head_norm(("qk", *norm_event(s - 1)))
                t, r = divmod(s, WINDOW)
                if t < TILES and r == 0:
                    if t:
                        pe.wait_ge(g_state, 2 * t)
                    for p in range(2):
                        last = nc.tensor.transpose(bank[6][:, P * p:P * p + P], gk_t[:, p, P * t:P * t + P], ident[:, :])
                    last.then_inc(g_turned, 1)
                if t < TILES and r == 2:
                    pe.wait_ge(g_turned_out, t + 1)
                    mm(bank[6][:, 0:256], glr_t[:, P * t:P * t + P], gate_w2[:, :], start=True, stop=True).then_inc(g_logit, 1)
                if t < TILES and r == 5:
                    pe.wait_ge(g_log, t + 1)
                    mm(bank[6][:, 0:256], suffix[:, :], log_g[:, :], start=True, stop=True)
                    for p in range(2):
                        last = mm(bank[6][:, 256 + 2 * p:258 + 2 * p], log_g[:, P * p:P * p + P], chunk_sel[:, :],
                                  start=True, stop=True)
                    last.then_inc(g_decay, 1)
                for c, slot in ((0, 7), (1, 9)):
                    if t < TILES and r == slot:
                        if c == 0:
                            pe.wait_ge(g_kdec, t + 1)
                            pe.wait_ge(gvr_in, 32 * (t + 1))
                        else:
                            pe.wait_ge(g_state, 2 * t + 1)
                        tok = slice(CHUNK * c, CHUNK * c + CHUNK)
                        for p in range(2):
                            last = mm(bank[6][:, 256 * p:256 * p + 256], k_dec[tok, P * p:P * p + P],
                                      gv_s[tok, 256 * p:256 * p + 256], start=True, stop=True)
                        last.then_inc(g_kv, 1)
                for c, slot in ((0, 9), (1, 11)):
                    if t < TILES and r == slot:
                        n = 2 * t + c
                        pe.wait_ge(g_state, n + 1)
                        if c == 0 and t:
                            pe.wait_ge(g_mixl, t)
                            pe.wait_ge(g_mixh, t)
                        for p in range(2):
                            last = mm(bank[5][64 * c:64 * c + 64, 256 * p:256 * p + 256],
                                      gq_t[:, p, CHUNK * n:CHUNK * n + CHUNK], state[n % 3][:, p, :], start=True, stop=True)
                        last.then_inc(g_o, 1)
                if t >= 1 and r == 3 and t <= TILES:
                    pe.wait_ge(g_go, t)
                    for p in range(GLA_HEADS):
                        last = nc.tensor.transpose(bank[5][:, P * p:P * p + P], go[:, P * p:P * p + P], ident[:, :])
                    last.then_inc(g_got, 1)

            def turn_v(t):
                pe.wait_ge(v_ready, t + 1)
                if t:
                    pe.wait_ge(vt_ready, t)
                rows = v_row[:, :].rearrange("p (d k) -> p k d", k=KT)
                for k in range(KT):
                    last = nc.tensor.transpose(bank[4 + k // 4][:, P * (k % 4):P * (k % 4 + 1)], rows[:, k, :],
                                               ident[:, :])
                last.then_inc(v_turned, 1)

            def route(t):
                pe.wait_ge(vt_ready, t + 1)
                if t:
                    pe.wait_ge(logit_out, t)
                for k in range(KT):
                    last = mm(bank[6][:, 0:LOGITS], v_t[:, k, :], router_w[:, k, :], start=k == 0, stop=k == KT - 1)
                last.then_inc(logit_done, 1)

            for t in range(TILES):
                a = W_ORDER[t]
                tok = slice(P * a, P * a + P)
                if t <= 4:
                    pe.wait_ge(mix_ready, 7 if t < 4 else 8)
                    pe.wait_ge(g_mixh, min(5 + t, TILES))
                    pe.wait_ge(g_mixl, min(5 + t, TILES))
                if t >= 2:
                    pe.wait_ge(h_ready, t - 1)
                for k in range(KT):
                    if t == 0 and k % 2 == 0:
                        pe.wait_ge(wo_l_ready, k // 2 + 1)
                    for half in range(2):
                        col = slice(HALF * half, HALF * half + HALF)
                        last = three(bank[2 * (t % 2) + half][:, :], mix_h[:, k, tok], mix_l[:, k, tok],
                                     wo_h[:, k, col], wo_l[:, k, col], start=k == 0, stop=k == KT - 1)
                last.then_inc(wo_done, 1)
                if t >= 1:
                    turn_v(t - 1)
                if t >= 2:
                    route(t - 2)
            route(TILES - 2)
            turn_v(TILES - 1)
            route(TILES - 1)
            pe.wait_ge(routed, TILES)
            for t in range(TILES):
                for b in range(t + 1):
                    mm(bank[7][:, EXPERTS * t:EXPERTS * (t + 1)], (before if b == t else ones_b)[:, :], chosen_any[:, b, :],
                       start=b == 0, stop=b == t)
            for b in range(TILES):
                last = mm(bank[7][:, EXPERTS * TILES:EXPERTS * (TILES + 1)], ones_b[:, :], chosen_any[:, b, :],
                          start=b == 0, stop=b == TILES - 1)
            last.then_inc(ranked, 1)
            pe.wait_ge(row_hot_ready, 1)
            pe.wait_ge(entries_ready, 1)
            for n in range(2 * TILES):
                last = mm(bank[4][:, 0:2 * MAX_BLOCKS], row_hot[:, n, :], entries[:, n, :, :].rearrange("p c b -> p (c b)"),
                          start=n == 0, stop=n == 2 * TILES - 1)
            last.then_inc(table_done, 1)

            def turn_rows(i):
                pe.wait_ge(rows_in, 16 * (i + 1))
                rows = xb[:, :].rearrange("p (d k) -> p k d", k=KT)
                for k in range(KT):
                    last = nc.tensor.transpose(bank[2 + k // 4][:, P * (k % 4):P * (k % 4 + 1)], rows[:, k, :], ident[:, :])
                last.then_inc(x_turned, 1)

            def gate_up(i, m0):
                count, slot0 = m0
                pe.wait_ge(xh_ready, i + 1)
                pe.wait_ge(xl_ready, i + 1)
                for j in range(4):
                    pe.wait_ge(ew_l_ready, count + j + 1)
                    wh = ew_h[(slot0 + j) % SPLIT][:, :].rearrange("p (k n) -> p k n", n=FF)
                    wl = ew_l[(slot0 + j) % SPLIT][:, :].rearrange("p (k n) -> p k n", n=FF)
                    for kk in range(4):
                        k = 4 * (j % 2) + kk
                        last = three(bank[j // 2][:, :], xb_h[:, k, :], xb_l[:, k, :], wh[:, kk, :], wl[:, kk, :],
                                     start=k == 0, stop=k == KT - 1)
                    last.then_inc(ew_used, 1)

            def turn_act(i):
                pe.wait_ge(act_done, i + 1)
                rows = act_row[:, :].rearrange("p (f k) -> p k f", k=FT)
                for k in range(FT):
                    last = nc.tensor.transpose(bank[4][:, P * k:P * k + P], rows[:, k, :], ident[:, :])
                last.then_inc(a_turned, 1)

            def down(i, m0, first=False):
                count, slot0 = m0
                pe.wait_ge(ah_ready, i + 1)
                pe.wait_ge(al_ready, i + 1)
                if not first:
                    pe.wait_ge(y_ready, i)
                for j in range(2):
                    pe.wait_ge(ew_l_ready, count + j + 1)
                    wh = ew_h[(slot0 + j) % SPLIT][:, :].rearrange("p (k n) -> p k n", n=D)
                    wl = ew_l[(slot0 + j) % SPLIT][:, :].rearrange("p (k n) -> p k n", n=D)
                    for kk in range(2):
                        k = 2 * j + kk
                        for half in range(2):
                            col = slice(HALF * half, HALF * half + HALF)
                            last = three(bank[5 + half][:, :], a_h[:, k, :], a_l[:, k, :], wh[:, kk, col], wl[:, kk, col],
                                         start=k == 0, stop=k == FT - 1)
                    last.then_inc(ew_used, 1)

            turn_rows(0)
            gate_up(0, (0, 0))
            pe.wait_ge(control_ready, 1)
            blocks = pe.value_load(control[0:1, 0:1], min_val=0, max_val=MAX_BLOCKS - 1 - EXPERTS) + EXPERTS
            turn_rows(1)
            turn_act(0)
            gate_up(1, (4, 4))
            turn_rows(2)
            down(0, (8, 2), first=True)
            turn_act(1)
            with pe.Fori(2, blocks - 1) as i:
                gate_up(i, (6 * i - 2, 4))
                turn_rows(i + 1)
                down(i - 1, (6 * i + 2, 2))
                turn_act(i)
            gate_up(blocks - 1, (6 * blocks - 8, 4))
            down(blocks - 2, (6 * blocks - 4, 2))
            turn_act(blocks - 1)
            down(blocks - 1, (6 * blocks - 2, 4))

        @block.scalar
        def _(act):
            chain = [0]

            def link(ins):
                chain[0] += 1
                ins.then_inc(asmall, 1)
                act.wait_ge(asmall, chain[0])

            A = nc.scalar.activation
            nc.scalar.preload_act_table_set("natural_log_exp_and_others")

            def rstd_of(dst, src, ln_bias=None):
                link(A(dst, src, ACT.Ln, bias=ln_bias) if ln_bias is not None else A(dst, src, ACT.Ln))
                return A(dst, dst, ACT.Exp, scale=-0.5)

            def split_win(n):
                act.wait_ge(win_in[n % 2], 16 * (n // 2 + 1))
                if n >= 2:
                    if n % 2 == 0:
                        act.wait_ge(win_used, n // 2)
                    else:
                        act.wait_ge(unit_done, 8 * (n // 2))
                A(win_h[n % 2][:, :, :].rearrange("p k n -> p (k n)"), win_raw[n % 2][:, :], ACT.Copy).then_inc(win_h_ready, 1)

            def u_high(t):
                act.wait_ge(u_turned, t + 1)
                for b in range(2):
                    last = A(u_h[:, 4 * b:4 * b + 4, P * t:P * t + P],
                             bank[2 * (t % 2) + b][:, :].rearrange("p (k n) -> p k n", n=P), ACT.Copy)
                last.then_inc(uh_ready, 1)

            def square_x(t):
                act.wait_ge(xs[t], 16)
                if t:
                    act.wait_ge(square_done, t)
                A(squares[:, :], x_in[t][:, :], ACT.Square, accum_out=row_sum[:, t:t + 1]).then_inc(square_done, 1)

            square_x(0)
            for t in range(TILES):
                if t + 1 < TILES:
                    square_x(t + 1)
                act.wait_ge(mean_done, t + 1)
                rstd_of(row_rstd[:, t:t + 1], row_mean[:, t:t + 1]).then_inc(rstd_done, 1)
                if t:
                    u_high(t - 1)
                if t == EARLY:
                    split_win(0)
            u_high(TILES - 1)
            split_win(1)
            n_spill = 0
            for c, name in enumerate(ORDER):
                if 2 * c + 2 < 2 * len(ORDER):
                    split_win(2 * c + 2)
                else:
                    act.wait_ge(glr_in, 16)
                    A(glr_h[:, :, :], glr_raw[:, :, :], ACT.Copy).then_inc(glr_split, 1)
                for u in range(8):
                    act.wait_ge(unit_done, 8 * c + u + 1)
                    src = unit_bank(u)[:, :]
                    if name in ("gv", "gr"):
                        slot = n_spill % 2
                        if n_spill >= 2:
                            act.wait_ge(spilled[slot], 16 * (n_spill // 2))
                        A(spill[slot][:, :], src, ACT.Copy).then_inc(unit_out, 1)
                        act.wait_ge(unit_out, 8 * c + u + 1)
                        act.dma_start((gv_dram if name == "gv" else gr_dram)[u], spill[slot][:, :]).then_inc(spilled[slot], 16)
                        n_spill += 1
                    elif name == "v":
                        A(v_s[:, u, :], src, ACT.Copy).then_inc(unit_out, 1)
                    else:
                        g, tok = u // 2, slice(HALF * (u % 2), HALF * (u % 2) + HALF)
                        if name == "gqk":
                            A((gq_t if g < 2 else gk_t)[:, g % 2, tok], src, ACT.Copy,
                              scale=GLA_K ** -0.5 if g < 2 else 1.0).then_inc(unit_out, 1)
                        else:
                            A((q_t if name == "q" else k_t)[:, g, tok], src, ACT.Copy).then_inc(unit_out, 1)
                if 2 * c + 3 < 2 * len(ORDER):
                    split_win(2 * c + 3)

            def norm_square(key):
                n = norm_order[key]
                if n >= 2:
                    act.wait_ge(ms_done, n - 1)
                if key[0] == "qk":
                    A(sq[n % 2][:, :], qk_block(key[2], key[1]), ACT.Square).then_inc(sq_done, 1)
                else:
                    g = key[1]
                    if g:
                        act.wait_ge(mix_ready, g)
                    A(o_s[:, :], bank[4][:, :], ACT.Copy).then_inc(o_out, 1)
                    act.wait_ge(o_out, g + 1)
                    A(sq[n % 2][:, :], o_s[:, :], ACT.Square).then_inc(sq_done, 1)

            def norm_rstd(key):
                n = norm_order[key]
                act.wait_ge(ms_done, n + 1)
                if n >= 2:
                    act.wait_ge(q_normed, used_norms[n - 1][0])
                    if used_norms[n - 1][1]:
                        act.wait_ge(mix_ready, used_norms[n - 1][1])
                A(rs[n % 2][:, :], bank[7][:, :], ACT.Ln, bias=eps_col[:, :]).then_inc(rln_done, 1)
                act.wait_ge(rln_done, n + 1)
                A(rs[n % 2][:, :], rs[n % 2][:, :], ACT.Exp, scale=-0.5).then_inc(rs_done, 1)

            used_norms = [(0, 0)]
            for key in sorted(norm_order, key=norm_order.get):
                qk, o = used_norms[-1]
                used_norms.append((qk + 1, o) if key[0] == "qk" else (qk, o + 1))

            act.wait_ge(fixed, 1)
            norm_square(("qk", 0, 0))
            for b in range(QN):
                if b + 1 < QN:
                    norm_square(("qk", 0, b + 1))
                norm_rstd(("qk", 0, b))
                if b < 2:
                    act.wait_ge(glr_ones, b + 1)
                    act.wait_ge(glr_done, b + 1)
                    A(glr_t[0:RANK, HALF * b:HALF * b + HALF], unit_bank(b)[0:RANK, :], ACT.Copy).then_inc(glr_out, 1)

            def wo_high(n):
                act.wait_ge(pv_done, NU)
                act.wait_ge(g_o, 2 * TILES)
                act.wait_ge(raw_in[n], 16)
                A(wo_h[:, 2 * n:2 * n + 2, :].rearrange("p k n -> p (k n)"), raw[n][:, :], ACT.Copy).then_inc(wo_h_ready, 1)

            for s in range(SLOT_END):
                if s >= 4 and s - 4 in GROUP_END:
                    act.wait_ge(pv_done, s - 3)
                    norm_square(("o", GROUP_END[s - 4]))
                if s < NU:
                    u = units[s]
                    w = soft[s % 2][:, u["lo"]:HALF]
                    act.wait_ge(qk_done, s + 1)
                    if s >= 2:
                        act.wait_ge(sp_done, s - 1)
                    link(A(w, bank[s % 4][:, u["lo"]:HALF], ACT.Abs))
                    link(A(w, w, ACT.Exp, scale=-1.0))
                    A(w, w, ACT.Ln, bias=1.0).then_inc(ln_done, 1)
                if 2 <= s and s - 2 < NU:
                    n, u = s - 2, units[s - 2]
                    act.wait_ge(tail_done, n + 1)
                    if n >= 2:
                        act.wait_ge(pv_done, n - 1)
                    A(prob[n % 2][:, u["lo"]:HALF], bank[n % 4][:, u["lo"]:HALF], ACT.Exp).then_inc(prob_done, 1)
                if s >= 6 and s - 6 in GROUP_END:
                    norm_rstd(("o", GROUP_END[s - 6]))
                if norm_event(s):
                    norm_square(("qk", *norm_event(s)))
                if s >= 2 and norm_event(s - 2):
                    norm_rstd(("qk", *norm_event(s - 2)))
                t, r = divmod(s, WINDOW)
                if t < TILES and r == 1:
                    act.wait_ge(g_turned, t + 1)
                    if t:
                        act.wait_ge(g_kdec, t)
                    A(gk_s[:, :], bank[6][:, 0:256], ACT.Copy).then_inc(g_turned_out, 1)
                if t < TILES and r == 3:
                    act.wait_ge(g_cap, t + 1)
                    link(A(log_g[:, :], log_g[:, :], ACT.Exp, scale=-1.0))
                    A(log_g[:, :], log_g[:, :], ACT.Ln, bias=1.0).then_inc(g_ln, 1)
                if t < TILES and r == 6:
                    act.wait_ge(g_decay, t + 1)
                    A(k_dec[:, :], bank[6][:, 0:256], ACT.Exp)
                    A(gstat[:, 0:4], bank[6][:, 256:260], ACT.Exp).then_inc(g_exp, 1)
                if t < TILES and r == 3:
                    act.wait_ge(g_rcap, t + 1)
                    A(gsig[:, :], gsig[:, :], ACT.Exp, scale=-1.0).then_inc(g_sig_part, 1)
                if t < TILES and r == 7:
                    act.wait_ge(g_sig_part, 2 * t + 1)
                    A(gsig[:, :], gsig[:, :], ACT.Ln, bias=1.0).then_inc(g_sig_part, 1)
                if t < TILES and r == 8:
                    act.wait_ge(g_sig_part, 2 * t + 2)
                    A(gsig[:, :], gsig[:, :], ACT.Exp, scale=-1.0).then_inc(g_sig, 1)
                if 1 <= t <= TILES and r == 0:
                    act.wait_ge(g_o, 2 * t)
                    if t >= 2:
                        act.wait_ge(g_got, t - 1)
                    A(go[:, :], bank[5][:, :], ACT.Square).then_inc(g_sq, 1)
                if 1 <= t <= TILES and r == 1:
                    act.wait_ge(g_ms, t)
                    rstd_of(gstat[:, 8:12], gstat[:, 12:16]).then_inc(g_rs, 1)
                if 1 <= t <= TILES and r == 7:
                    act.wait_ge(g_got, t)
                    A(mix_h[:, 4:8, P * (t - 1):P * t], bank[5][:, :].rearrange("p (k n) -> p k n", n=P),
                      ACT.Copy).then_inc(g_mixh, 1)

                if s - DRAIN in range(WO_EARLY):
                    wo_high(s - DRAIN)

            for n in range(WO_EARLY, 4):
                wo_high(n)
            for t in range(TILES + 2):
                if t < TILES:
                    act.wait_ge(h_ready, t + 1)
                    if t:
                        act.wait_ge(v_turned, t)
                        act.wait_ge(v_stored, 16 * t)
                    A(v_row[:, :], h_row[t % 2][:, :], ACT.Square, accum_out=stat[:, 3:4]).then_inc(h_square, 1)
                    act.wait_ge(h_mean, t + 1)
                    rstd_of(stat[:, 5:6], stat[:, 4:5]).then_inc(h_rstd, 1)
                if 1 <= t <= TILES:
                    act.wait_ge(v_turned, t)
                    if t >= 2:
                        act.wait_ge(logit_done, t - 1)
                    for b in range(2):
                        last = A(v_t[:, 4 * b:4 * b + 4, :], bank[4 + b][:, :].rearrange("p (k n) -> p k n", n=P), ACT.Copy)
                    last.then_inc(vt_ready, 1)
                if t >= 2:
                    act.wait_ge(r_max, t - 1)
                    A(r_small[:, 0:N_GROUPS], grp_logits[:, 0:N_GROUPS], ACT.Exp, bias=stat[:, 6:7],
                      accum_out=stat[:, 7:8]).then_inc(r_exp, 1)
                    act.wait_ge(r_diff, t - 1)
                    A(stat[:, 9:10], stat[:, 8:9], ACT.Exp).then_inc(r_ratio, 1)

            def high(count, slot, raw_slot, uses, guard=True):
                act.wait_ge(raw_in[raw_slot], 16 * uses)
                if guard:
                    act.wait_ge(ew_used, count - SPLIT + 1)
                A(ew_h[slot % SPLIT][:, :], raw[raw_slot][:, :], ACT.Copy).then_inc(ew_h_ready, 1)

            def x_high(i):
                act.wait_ge(x_turned, i + 1)
                for b in range(2):
                    last = A(xb_h[:, 4 * b:4 * b + 4, :], bank[2 + b][:, :].rearrange("p (k n) -> p k n", n=P), ACT.Copy)
                last.then_inc(xh_ready, 1)

            def silu_of(i):
                act.wait_ge(gate_or_up(i, 2)[0], gate_or_up(i, 2)[1])
                A(silu[:, :], bank[0][:, :], ACT.Silu).then_inc(silu_done, 1)

            def gate_or_up(i, j):
                return ew_used, used_before(i) + j

            def used_before(i):
                return 0 if isinstance(i, int) and i == 0 else (4 if isinstance(i, int) and i == 1 else 6 * i - 2)

            def back(i):
                act.wait_ge(down_count, down_value(i))
                act.wait_ge(row_ready, i + 1)
                for b in range(2):
                    last = A(y_row[:, HALF * b:HALF * b + HALF], bank[5 + b][:, :], ACT.Copy,
                             scale=scatter_row[:, 1:2].bitcast(fp32))
                last.then_inc(y_ready, 1)

            down_count = ew_used

            def down_value(i):
                return 6 * i + 10

            def a_high(i):
                act.wait_ge(a_turned, i + 1)
                A(a_h[:, :, :], bank[4][:, :].rearrange("p (k n) -> p k n", n=P), ACT.Copy).then_inc(ah_ready, 1)

            act.wait_ge(wo_done, TILES)
            for m in range(4):
                high(m, m, raw_slot(m), raw_count(m), guard=False)
            for j in range(2):
                high(4 + j, 4 + j, raw_slot(4 + j), raw_count(4 + j), guard=False)
            x_high(0)
            act.wait_ge(control_ready, 1)
            blocks = act.value_load(control[0:1, 0:1], min_val=0, max_val=MAX_BLOCKS - 1 - EXPERTS) + EXPERTS
            for j in range(2, 4):
                high(4 + j, 4 + j, raw_slot(4 + j), raw_count(4 + j))
                if j == 2:
                    silu_of(0)
            x_high(1)
            for j in range(4, 6):
                high(4 + j, 4 + j, raw_slot(4 + j), raw_count(4 + j))
            a_high(0)

            def step(i, last=False):
                def piece(j):
                    if isinstance(i, int):
                        high(6 * i + 4 + j, 4 + j, raw_slot(6 * i + 4 + j), raw_count(6 * i + 4 + j))
                    else:
                        high(6 * i + 4 + j, 4 + j, j, i - 2 + raw_count(16 + j))
                if not last:
                    for j in range(2):
                        piece(j)
                if last:
                    high(6 * i + 4, 4, 0, i - 2 + raw_count(16))
                silu_of(i)
                if not last:
                    for j in range(2, 4):
                        piece(j)
                    x_high(i + 1)
                if last:
                    high(6 * i + 5, 5, 1, i - 2 + raw_count(17))
                else:
                    for j in range(4, 6):
                        piece(j)
                back(i - 1)
                a_high(i)

            step(1)
            with act.Fori(2, blocks - 1) as i:
                step(i)
            step(blocks - 1, last=True)
            act.wait_ge(ew_used, 6 * blocks)
            act.wait_ge(row_ready, blocks)
            for b in range(2):
                last = A(y_row[:, HALF * b:HALF * b + HALF], bank[5 + b][:, :], ACT.Copy,
                         scale=scatter_row[:, 1:2].bitcast(fp32))
            last.then_inc(y_ready, 1)

        @block.vector
        def _(dve):
            V = nc.vector
            chain = [0]

            def link(ins):
                chain[0] += 1
                ins.then_inc(small, 1)
                dve.wait_ge(small, chain[0])

            def low(dst, src, high):
                return V.tensor_tensor(dst, src, high.bitcast(fp32), SUB)

            dve.wait_ge(fixed, 1)
            V.tensor_copy(ident_b[:, :], ident[:, :])
            V.tensor_copy(tri_neg[:, :], tri_f[:, :]).then_inc(fixed, 1)

            def u_low(t):
                dve.wait_ge(uh_ready, t + 1)
                for b in range(2):
                    dst = (slice(None), slice(4 * b, 4 * b + 4), slice(P * t, P * t + P))
                    last = low(u_l[dst], bank[2 * (t % 2) + b][:, :].rearrange("p (k n) -> p k n", n=P), u_h[dst])
                last.then_inc(ul_ready, 1)

            def win_low(n):
                dve.wait_ge(win_h_ready, n + 1)
                low(win_l[n % 2][:, :, :].rearrange("p k n -> p (k n)"), win_raw[n % 2][:, :],
                    win_h[n % 2][:, :, :].rearrange("p k n -> p (k n)")).then_inc(win_l_ready, 1)

            def mean_of(t):
                dve.wait_ge(square_done, t + 1)
                V.tensor_scalar(row_mean[:, t:t + 1], row_sum[:, t:t + 1], 1.0 / D, EPS, MUL, ADD).then_inc(mean_done, 1)

            mean_of(0)
            dve.wait_ge(gain_in, 16)
            for t in range(TILES):
                if t + 1 < TILES:
                    mean_of(t + 1)
                dve.wait_ge(rstd_done, t + 1)
                if t >= 2:
                    dve.wait_ge(u_turned, t - 1)
                if t == 0:
                    V.scalar_tensor_tensor(out=u_row[0][:, :], in0=x_in[0][:, :], scalar=row_rstd[:, 0:1], in1=gain1[:, :],
                                           op0=MUL, op1=MUL).then_inc(u_ready, 1)
                else:
                    dve.wait_ge(x_gained, t)
                    V.tensor_scalar(u_row[t % 2][:, :], x_in[t][:, :], row_rstd[:, t:t + 1], None, MUL).then_inc(u_ready, 1)
                if t:
                    u_low(t - 1)
                if t == EARLY:
                    win_low(0)

            u_low(TILES - 1)
            for n in range(1, 2 * len(ORDER)):
                win_low(n)
            dve.wait_ge(glr_split, 1)
            low(glr_l[:, :, :], glr_raw[:, :, :], glr_h[:, :, :]).then_inc(glr_split, 1)
            dve.wait_ge(consts_in, 16 * (N_CONSTS + 1))
            link(V.tensor_scalar(q_gain[:, :], q_gain[:, :], SB_DIM ** -0.5, None, MUL))

            def norm_qk(pair, b):
                dve.wait_ge(rs_done, norm_order[("qk", pair, b)] + 1)
                blk_ap = qk_block(b, pair)
                V.scalar_tensor_tensor(out=blk_ap, in0=blk_ap, scalar=(q_gain if b < 2 else k_gain)[:, :], in1=rs[norm_order[("qk", pair, b)] % 2][:, :],
                                       op0=MUL, op1=MUL).then_inc(q_normed, 1)

            for b in range(QN):
                if b < 2:
                    dve.wait_ge(glr_done, b + 1)
                    V.memset(glr_t[:, HALF * b:HALF * b + HALF], 1.0).then_inc(glr_ones, 1)
                norm_qk(0, b)

            def wo_low(n):
                dve.wait_ge(wo_h_ready, n + 1)
                cols = (slice(None), slice(2 * n, 2 * n + 2), slice(None))
                low(wo_l[cols].rearrange("p k n -> p (k n)"), raw[n][:, :], wo_h[cols].rearrange("p k n -> p (k n)")).then_inc(
                    wo_l_ready, 1)

            for s in range(SLOT_END):
                if 1 <= s <= NU:
                    n, u = s - 1, units[s - 1]
                    cols = slice(u["lo"], HALF)
                    dve.wait_ge(ln_done, n + 1)
                    if n >= 3:
                        dve.wait_ge(later_done, laters(n - 2))
                    V.scalar_tensor_tensor(out=sp[n % 3][:, cols], in0=bank[n % 4][:, cols], scalar=0.0,
                                           in1=soft[n % 2][:, cols], op0=ALU.max, op1=ADD).then_inc(sp_done, 1)
                    dve.wait_ge(sp_done, n + 1)
                    if n >= 3:
                        dve.wait_ge(tail_done, n - 2)
                    link(V.tensor_copy(sp_h[n % 3][:, cols], sp[n % 3][:, cols]))
                    low(sp_l[n % 3][:, cols], sp[n % 3][:, cols], sp_h[n % 3][:, cols]).then_inc(spl_done, 1)
                if s >= 7 and s - 7 in GROUP_END:
                    g = GROUP_END[s - 7]
                    pair, q0 = g // 2, HALF * (1 - g % 2)
                    dve.wait_ge(rs_done, norm_order[("o", g)] + 1)
                    link(V.scalar_tensor_tensor(out=o_s[:, :], in0=o_s[:, :], scalar=o_gain[:, pair:pair + 1],
                                                in1=rs[norm_order[("o", g)] % 2][:, :],
                                                op0=MUL, op1=MUL))
                    dst = (slice(None), pair, slice(q0, q0 + HALF))
                    link(V.tensor_copy(mix_h[dst], o_s[:, :]))
                    low(mix_l[dst], o_s[:, :], mix_h[dst]).then_inc(mix_ready, 1)
                if s >= 3 and norm_event(s - 3):
                    norm_qk(*norm_event(s - 3))
                t, r = divmod(s, WINDOW)
                if 1 <= t <= TILES and r == 0:
                    dve.wait_ge(g_sq, t)
                    link(V.reduce_sum(gstat[:, 4:8], go[:, :].rearrange("p (h n) -> p h n", n=GLA_V), axis=AX.X))
                    V.tensor_scalar(gstat[:, 12:16], gstat[:, 4:8], 1.0 / GLA_V, EPS, MUL, ADD).then_inc(g_ms, 1)
                if 1 <= t <= TILES and r == 2:
                    dve.wait_ge(g_rs, t)
                    dve.wait_ge(g_gain, t)
                    for h in range(GLA_HEADS):
                        c = slice(GLA_V * h, GLA_V * (h + 1))
                        last = V.scalar_tensor_tensor(out=go[:, c], in0=bank[5][:, c], scalar=gstat[:, 8 + h:9 + h],
                                                      in1=gsig[:, c], op0=MUL, op1=MUL)
                    last.then_inc(g_go, 1)
                if t < TILES and r == 2:
                    if t:
                        dve.wait_ge(g_go, t)
                    dve.wait_ge(gvr_in, 32 * (t + 1))
                    V.tensor_scalar(gsig[:, :], gr_s[:, :], -GUARD, None, ALU.max).then_inc(g_rcap, 1)
                if t < TILES and r == 3:
                    dve.wait_ge(g_logit, t + 1)
                    if t:
                        dve.wait_ge(g_decay, t)
                    V.tensor_scalar(log_g[:, :], bank[6][:, 0:256], -CAP, None, ALU.max).then_inc(g_cap, 1)
                if t < TILES and r == 9:
                    dve.wait_ge(g_sig, t + 1)
                    V.tensor_tensor(gsig[:, :], gsig[:, :], gr_s[:, :], MUL).then_inc(g_silu, 1)
                if t < TILES and r == 4:
                    dve.wait_ge(g_ln, t + 1)
                    V.scalar_tensor_tensor(out=log_g[:, :], in0=log_g[:, :], scalar=-1.0, in1=bank[6][:, 0:256],
                                           op0=MUL, op1=ALU.min).then_inc(g_log, 1)
                if t < TILES and r == 6:
                    dve.wait_ge(g_exp, t + 1)
                    V.tensor_tensor(k_dec[:, :], k_dec[:, :], gk_s[:, :], MUL).then_inc(g_kdec, 1)
                for c, slot in ((0, 8), (1, 10)):
                    if t < TILES and r == slot:
                        n = 2 * t + c
                        dve.wait_ge(g_kv, n + 1)
                        if n >= 3:
                            dve.wait_ge(g_o, n - 2)
                        for p in range(2):
                            for h in range(2):
                                row, col = slice(64 * h, 64 * h + 64), slice(GLA_V * h, GLA_V * (h + 1))
                                last = V.scalar_tensor_tensor(
                                    out=state[n % 3][row, p, col], in0=state[(n - 1) % 3][row, p, col],
                                    scalar=gstat[row, 2 * p + c:2 * p + c + 1],
                                    in1=bank[6][row, 256 * p + GLA_V * h:256 * p + GLA_V * (h + 1)], op0=MUL, op1=ADD)
                        last.then_inc(g_state, 1)
                        dve.wait_ge(g_state, n + 1)
                if 1 <= t <= TILES and r == 8:
                    dve.wait_ge(g_mixh, t)
                    dst = (slice(None), slice(4, 8), slice(P * (t - 1), P * t))
                    low(mix_l[dst], bank[5][:, :].rearrange("p (k n) -> p k n", n=P), mix_h[dst]).then_inc(g_mixl, 1)

                if s - DRAIN - 1 in range(WO_EARLY):
                    wo_low(s - DRAIN - 1)

            for n in range(WO_EARLY, 4):
                wo_low(n)
            dve.wait_ge(gain2_in, 16)
            for t in range(TILES + 2):
                if t < TILES:
                    dve.wait_ge(wo_done, t + 1)
                    dve.wait_ge(hx[t % 2], 16 * (t // 2 + 1))
                    for b in range(2):
                        c = slice(HALF * b, HALF * b + HALF)
                        last = V.tensor_tensor(h_row[t % 2][:, c], h_row[t % 2][:, c], bank[2 * (t % 2) + b][:, :], ADD)
                    last.then_inc(h_ready, 1)
                    dve.wait_ge(h_square, t + 1)
                    V.tensor_scalar(stat[:, 4:5], stat[:, 3:4], 1.0 / D, EPS, MUL, ADD).then_inc(h_mean, 1)
                    dve.wait_ge(h_rstd, t + 1)
                    V.scalar_tensor_tensor(out=v_row[:, :], in0=h_row[t % 2][:, :], scalar=stat[:, 5:6], in1=gain2[:, :],
                                           op0=MUL, op1=MUL).then_inc(v_ready, 1)
                if t >= 2:
                    n, a = t - 2, W_ORDER[t - 2]
                    dve.wait_ge(logit_done, n + 1)
                    V.tensor_tensor(grp_logits[:, 0:N_GROUPS], bank[6][:, 0:N_GROUPS], router_bias[:, 0:N_GROUPS], ADD)
                    last = V.tensor_tensor(exp_logits[:, :], bank[6][:, N_GROUPS:LOGITS], router_bias[:, N_GROUPS:LOGITS], ADD)
                    last.then_inc(logit_out, 1)
                    dve.wait_ge(logit_out, n + 1)
                    link(V.max(top_val[:, 0, :], grp_logits[:, :]))
                    link(V.max_index(top_idx[:, 0, :], top_val[:, 0, :], grp_logits[:, :]))
                    V.tensor_scalar(stat[:, 6:7], top_val[:, 0, 0:1], -1.0, None, MUL).then_inc(r_max, 1)
                    link(V.tensor_copy(r_small[:, 8:9], top_idx[:, 0, 0:1]))
                    link(V.tensor_scalar(r_small[:, 12:16], iota[:, 0:N_GROUPS], r_small[:, 8:9], None, ALU.is_equal))
                    link(V.tensor_tensor(masked[:, :].rearrange("p (e g) -> p e g", g=N_GROUPS),
                                         exp_logits[:, :].rearrange("p (g e) -> p e g", g=N_GROUPS),
                                         r_small[:, 12:16].rearrange("p (a g) -> p a g", a=1).broadcast_to(
                                             [P, PER_GROUP, N_GROUPS]), MUL))
                    link(V.reduce_sum(sel_logits[:, :], masked[:, :].rearrange("p (e g) -> p e g", g=N_GROUPS), axis=AX.X))
                    link(V.max(top_val[:, 1, :], sel_logits[:, :]))
                    link(V.max_index(top_idx[:, 1, :], top_val[:, 1, :], sel_logits[:, :]))
                    V.tensor_tensor(stat[:, 8:9], top_val[:, 1, 1:2], top_val[:, 1, 0:1], SUB).then_inc(r_diff, 1)
                    link(V.tensor_copy(r_small[:, 16:18], top_idx[:, 1, 0:2]))
                    link(V.scalar_tensor_tensor(out=expert_of[:, a, :], in0=r_small[:, 8:9].broadcast_to([P, 2]),
                                                scalar=float(PER_GROUP), in1=r_small[:, 16:18], op0=MUL, op1=ADD))
                    for j in range(2):
                        last = V.tensor_scalar(chosen[:, a, j, :], iota[:, 0:EXPERTS], expert_of[:, a, j:j + 1], None, ALU.is_equal)
                    link(last)
                    link(V.tensor_tensor(chosen_any[:, a, :], chosen[:, a, 0, :], chosen[:, a, 1, :], ADD))
                    dve.wait_ge(r_exp, n + 1)
                    dve.wait_ge(r_ratio, n + 1)
                    link(V.scalar_tensor_tensor(out=stat[:, 10:11], in0=stat[:, 9:10], scalar=1.0, in1=stat[:, 7:8],
                                                op0=ADD, op1=MUL))
                    link(V.reciprocal(stat[:, 11:12], stat[:, 10:11]))
                    gates = payload[:, a, :, 1]
                    V.tensor_copy(gates[:, 0:1], stat[:, 11:12])
                    V.tensor_tensor(gates[:, 1:2], stat[:, 11:12], stat[:, 9:10], MUL).then_inc(routed, 1)
                    dve.wait_ge(routed, n + 1)

            V.memset(xb[:, :], 0.0).then_inc(xb_clear, 1)

            def of_assignment(small_ap, width):
                return small_ap.rearrange("p (n a) -> p n a", a=1).broadcast_to([P, 2 * TILES, width])

            def per_row(ap, width, n=2 * TILES):
                return ap.rearrange("p (a e) -> p a e", a=1).broadcast_to([P, n, width])

            chosen_v = chosen[:, :, :, :].rearrange("p t j e -> p (t j) e")
            product = by_expert[:, :].rearrange("p (n e) -> p n e", e=EXPERTS)
            over_v = over[:, :].rearrange("p (e m) -> p e m", m=STEPS)
            over_row_v = over_row[:, :].rearrange("p (n m) -> p n m", m=STEPS)
            dve.wait_ge(ranked, 1)
            counts = bank[7][:, EXPERTS * TILES:EXPERTS * (TILES + 1)]
            V.tensor_tensor(over_v, counts.rearrange("p (e a) -> p e a", a=1).broadcast_to([P, EXPERTS, STEPS]),
                            per_row(steps[:, :], STEPS, EXPERTS), ALU.is_gt)
            link(V.tensor_tensor(by_expert[:, :].rearrange("p (t j e) -> p t j e", j=2, e=EXPERTS),
                                 bank[7][:, 0:EXPERTS * TILES].rearrange("p (t a e) -> p t a e", a=1, e=EXPERTS).broadcast_to(
                                     [P, TILES, 2, EXPERTS]), chosen[:, :, :, :], MUL))
            V.reduce_sum(n_extra[:, :], over_v, axis=AX.X)
            link(V.reduce_sum(rank[:, :], product, axis=AX.X))
            V.tensor_tensor_scan(out=end_extra[:, :], data0=zeros[:, :], data1=n_extra[:, :], initial=0.0, op0=ADD, op1=ADD)
            link(V.tensor_tensor(over_row_v, of_assignment(rank[:, :], STEPS), per_row(steps[:, :], STEPS), ALU.is_ge))
            V.tensor_tensor(start_extra[:, :], end_extra[:, :], n_extra[:, :], SUB)
            link(V.reduce_sum(level[:, :], over_row_v, axis=AX.X))
            V.scalar_tensor_tensor(out=block_row[:, :], in0=level[:, :], scalar=-float(P), in1=rank[:, :], op0=MUL,
                                   op1=ADD)
            link(V.tensor_tensor(product, per_row(start_extra[:, :], EXPERTS), chosen_v, MUL))
            V.tensor_tensor(row_hot[:, :, :], per_row(iota[:, :], P), of_assignment(block_row[:, :], P),
                            ALU.is_equal).then_inc(row_hot_ready, 1)
            link(V.reduce_sum(extra[:, :], product, axis=AX.X))
            link(V.scalar_tensor_tensor(out=blk[:, :], in0=level[:, :], scalar=float(EXPERTS - 1), in1=extra[:, :],
                                        op0=ADD, op1=ADD))
            link(V.tensor_tensor(moved[:, :], expert_of[:, :, :].rearrange("p t j -> p (t j)"), blk[:, :], SUB))
            link(V.scalar_tensor_tensor(out=moved[:, :], in0=level[:, :], scalar=0.0, in1=moved[:, :], op0=ALU.is_equal,
                                        op1=MUL))
            link(V.tensor_tensor(blk[:, :], blk[:, :], moved[:, :], ADD))
            link(V.tensor_tensor(block_hot[:, :, :], per_row(iota[:, 0:MAX_BLOCKS], MAX_BLOCKS),
                                 of_assignment(blk[:, :], MAX_BLOCKS), ALU.is_equal))
            for c in range(2):
                last = V.tensor_tensor(entries[:, :, c, :], block_hot[:, :, :],
                                       payload[:, :, :, c:c + 1].rearrange("p t j c -> p (t j) c").broadcast_to(
                                           [P, 2 * TILES, MAX_BLOCKS]), MUL)
            last.then_inc(entries_ready, 1)
            ends = by_expert[:, :].rearrange("p (b e) -> p b e", e=EXPERTS)
            link(V.tensor_tensor(ends, per_row(end_extra[:, :], EXPERTS),
                                 iota[:, 0:16].rearrange("p (b a) -> p b a", a=1).broadcast_to([P, 16, EXPERTS]), ALU.is_le))
            link(V.reduce_sum(ctl_f[:, 2:18], ends, axis=AX.X))
            V.memset(ctl_f[:, 1:2], float(EXPERTS - 1))
            V.memset(ctl_f[:, 18 + EXPERTS:18 + MAX_BLOCKS], 2.0)
            link(V.tensor_scalar(ctl_f[:, 18:18 + EXPERTS], counts, float(MOVED[0]), None, ALU.is_gt))
            V.scalar_tensor_tensor(out=ctl_f[:, 18:18 + EXPERTS], in0=counts, scalar=float(MOVED[1]),
                                   in1=ctl_f[:, 18:18 + EXPERTS], op0=ALU.is_gt, op1=ADD)
            V.tensor_copy(ctl_f[:, 0:1], end_extra[:, EXPERTS - 1:EXPERTS])
            link(V.tensor_scalar(ctl_f[:, 2:18], ctl_f[:, 2:18], float(EXPERTS - 1), None, ALU.min))
            dve.wait_ge(table_done, 1)
            V.tensor_copy(table[:, :, 1].bitcast(fp32), bank[4][:, MAX_BLOCKS:2 * MAX_BLOCKS])
            V.tensor_scalar(table[:, :, 0].bitcast(i32), bank[4][:, 0:MAX_BLOCKS], -1.0, float(T), MUL,
                            ADD).then_inc(table_ready, 1)
            V.tensor_copy(control[:, :], ctl_f[:, :]).then_inc(control_ready, 1)

            def low_piece(count, slot, raw_slot):
                dve.wait_ge(ew_h_ready, count + 1)
                low(ew_l[slot % SPLIT][:, :], raw[raw_slot][:, :], ew_h[slot % SPLIT][:, :]).then_inc(ew_l_ready, 1)

            def x_low(i):
                dve.wait_ge(xh_ready, i + 1)
                for b in range(2):
                    last = low(xb_l[:, 4 * b:4 * b + 4, :], bank[2 + b][:, :].rearrange("p (k n) -> p k n", n=P),
                               xb_h[:, 4 * b:4 * b + 4, :])
                last.then_inc(xl_ready, 1)

            def activate(i, used):
                dve.wait_ge(silu_done, i + 1)
                dve.wait_ge(ew_used, used)
                V.tensor_tensor(act_row[:, :], silu[:, :], bank[1][:, :], MUL).then_inc(act_done, 1)

            def a_low(i):
                dve.wait_ge(ah_ready, i + 1)
                low(a_l[:, :, :], bank[4][:, :].rearrange("p (k n) -> p k n", n=P), a_h[:, :, :]).then_inc(al_ready, 1)

            dve.wait_ge(ew_l_ready, 4)
            for j in range(2):
                low_piece(4 + j, 4 + j, raw_slot(4 + j))
            dve.wait_ge(control_ready, 1)
            blocks = dve.value_load(control[0:1, 0:1], min_val=0, max_val=MAX_BLOCKS - 1 - EXPERTS) + EXPERTS
            x_low(0)
            for j in range(2, 4):
                low_piece(4 + j, 4 + j, raw_slot(4 + j))
                if j == 2:
                    activate(0, 4)
            x_low(1)
            for j in range(4, 6):
                low_piece(4 + j, 4 + j, raw_slot(4 + j))
            a_low(0)

            def step(i, last=False):
                def slot(j):
                    return raw_slot(6 * i + 4 + j) if isinstance(i, int) else j

                if not last:
                    for j in range(3):
                        low_piece(6 * i + 4 + j, 4 + j, slot(j))
                if last:
                    low_piece(6 * i + 4, 4, 0)
                activate(i, 6 * i + 2)
                if not last:
                    low_piece(6 * i + 7, 7, slot(3))
                    x_low(i + 1)
                if last:
                    low_piece(6 * i + 5, 5, 1)
                else:
                    for j in range(4, 6):
                        low_piece(6 * i + 4 + j, 4 + j, slot(j))
                a_low(i)

            step(1)
            with dve.Fori(2, blocks - 1) as i:
                step(i)
            step(blocks - 1, last=True)


_INS = ["x", "attn_norm_g", "w_in", "sb_q_norm_g", "sb_k_norm_g", "sb_out_norm_g", "gla_gate_w2", "gla_gate_b",
        "gla_out_norm_g", "w_out", "ffn_norm_g", "router_group_w", "router_group_b", "router_expert_w",
        "router_expert_b", "expert_w_gate", "expert_w_up", "expert_w_down"]


def kernel(**inputs):
    import numpy as _np
    import concourse.bacc as _bacc
    from concourse import mybir as _mybir
    from concourse.bass_utils import run_bass_kernel_spmd as _run

    nc = _bacc.Bacc("TRN2", target_bir_lowering=False, num_devices=1)
    arrays, args = {}, []
    for name in _INS:
        a = _np.ascontiguousarray(inputs[name])
        arrays[f"in_{name}"] = a
        args.append(nc.dram_tensor(f"in_{name}", a.shape, _mybir.dt.from_np(a.dtype), kind="ExternalInput").ap())
    out = nc.dram_tensor("out_dram", (1, T, D), _mybir.dt.float32, kind="ExternalOutput").ap()
    hybrid_block_kernel(nc, *args, out)
    r = _run(nc, [arrays], core_ids=[0])
    return r.results[0]["out_dram"]
```
